# Optimizing a Trainium2 kernel written in Bass

```python
import math
import jax, jax.numpy as jnp
from jax import lax
import numpy as np

D_MODEL = 1024
BATCH = 1
SEQ = 512
DEPTH = 1

HEAD_DIM = 64
D_ATTN = D_MODEL // 2
N_ATTN_HEADS = D_ATTN // HEAD_DIM
D_RNN = D_MODEL - D_ATTN
LRU_BLOCK = 64
N_LRU_BLOCKS = D_RNN // LRU_BLOCK
D_MIX = D_ATTN + D_RNN
D_IN_PROJ = 3 * D_ATTN + 2 * D_RNN
DILATED_PATTERNS = ((128, 1), (512, 4), (2048, 16))
ATTN_BLOCK = 128
CONV_WIDTH = 4
LRU_C = 8.0
D_FF = 2816
FFN_RES_WEIGHT = 0.5
N_SUBLAYERS = 3
RMS_EPS = 1e-6

kernel_name = "hybrid_dilated_attn_rglru_macaron_block"

def _rms(x):
    xf = x.astype(jnp.float32)
    return xf * lax.rsqrt(jnp.mean(xf * xf, axis=-1, keepdims=True) + RMS_EPS)

def _pre(x, g, shift, scale):
    return (_rms(x) * g * (1.0 + scale[:, None, :]) + shift[:, None, :]).astype(x.dtype)

def _post_residual(x, y, g, gate, weight):
    return x + (weight * (1.0 + gate[:, None, :]) * _rms(y) * g).astype(x.dtype)

def _swiglu(h, w_in, w_out):
    hg, hu = jnp.split(h @ w_in, 2, axis=-1)
    return (jax.nn.silu(hg) * hu) @ w_out

def _dilated_band(q, k, v, window, dilation):
    B, S, H, Dh = q.shape
    n_back = window // dilation
    chunk = dilation * ATTN_BLOCK
    s_pad = -(-S // chunk) * chunk
    L = s_pad // dilation
    nb = L // ATTN_BLOCK

    def to_strided(t):
        t = jnp.pad(t, ((0, 0), (0, s_pad - S), (0, 0), (0, 0)))
        t = t.reshape(B, L, dilation, H, Dh).transpose(0, 2, 1, 3, 4)
        return t.reshape(B, dilation, nb, ATTN_BLOCK, H, Dh)

    qs, ks, vs = to_strided(q), to_strided(k), to_strided(v)

    def with_prev(t):
        prev = jnp.pad(t[:, :, :-1], ((0, 0), (0, 0), (1, 0), (0, 0), (0, 0), (0, 0)))
        return jnp.concatenate([prev, t], axis=3)

    kk, vv = with_prev(ks), with_prev(vs)
    scores = jnp.einsum('brnqhd,brnkhd->brnhqk', qs, kk,
                        preferred_element_type=jnp.float32) * (Dh ** -0.5)
    qi = jnp.arange(ATTN_BLOCK)[:, None] + ATTN_BLOCK
    kj = jnp.arange(2 * ATTN_BLOCK)[None, :]
    dist = qi - kj
    band = (dist >= 0) & (dist <= n_back)
    has_prev = (jnp.arange(nb) > 0)[:, None, None] | (kj >= ATTN_BLOCK)[None]
    mask = (band[None] & has_prev)[:, None]
    scores = jnp.where(mask, scores, -jnp.inf)
    m = jnp.max(scores, axis=-1)
    p = jnp.exp(scores - m[..., None])
    l = jnp.sum(p, axis=-1)
    o = jnp.einsum('brnhqk,brnkhd->brnqhd', p, vv.astype(jnp.float32))

    def from_strided(t):
        X = t.shape[-1]
        t = t.reshape(B, dilation, L, H, X).transpose(0, 2, 1, 3, 4).reshape(B, s_pad, H, X)
        return t[:, :S]

    stats = from_strided(jnp.swapaxes(jnp.stack([m, l], axis=-1), 3, 4))
    return from_strided(o), stats[..., 0], stats[..., 1]

def _dilated_attention(q, k, v):
    res = [_dilated_band(q, k, v, w, d) for (w, d) in DILATED_PATTERNS]
    m_max = jnp.max(jnp.stack([r[1] for r in res]), axis=0)
    rescale = [jnp.exp(r[1] - m_max) for r in res]
    num = res[0][0] * rescale[0][..., None]
    den = res[0][2] * rescale[0]
    for r, s in zip(res[1:], rescale[1:]):
        num = num + r[0] * s[..., None]
        den = den + r[2] * s
    return num / den[..., None]

def _blockdiag(x, w):
    xb = x.reshape(x.shape[:-1] + (w.shape[0], w.shape[1]))
    return jnp.einsum('bsgi,gij->bsgj', xb, w).reshape(x.shape)

def _rg_lru(x, w_x, b_x, w_a, b_a, lam):
    f32 = jnp.float32
    xf = x.astype(f32)
    gate_x = jax.nn.sigmoid(_blockdiag(xf, w_x.astype(f32)) + b_x.astype(f32))
    gate_a = jax.nn.sigmoid(_blockdiag(xf, w_a.astype(f32)) + b_a.astype(f32))
    log_a = -LRU_C * gate_a * jax.nn.softplus(-lam.astype(f32))
    a = jnp.exp(log_a)
    b = xf * gate_x * jnp.sqrt(-jnp.expm1(2.0 * log_a))

    def combine(lhs, rhs):
        a_l, b_l = lhs
        a_r, b_r = rhs
        return a_l * a_r, a_r * b_l + b_r

    _, h = lax.associative_scan(combine, (a, b), axis=1)
    return h

def _hybrid_mixer(h, w_in, conv_w, conv_b, lru_w_x, lru_b_x, lru_w_a, lru_b_a, lru_lambda, w_out):
    B, S, _ = h.shape
    z = h @ w_in
    q, k, v, xr, gr = jnp.split(
        z, [D_ATTN, 2 * D_ATTN, 3 * D_ATTN, 3 * D_ATTN + D_RNN], axis=-1)
    heads = lambda t: t.reshape(B, S, N_ATTN_HEADS, HEAD_DIM)
    attn = _dilated_attention(heads(q), heads(k), heads(v)).reshape(B, S, D_ATTN)
    xr = lax.conv_general_dilated(
        xr, conv_w[:, None, :], window_strides=(1,), padding=[(CONV_WIDTH - 1, 0)],
        dimension_numbers=('NWC', 'WIO', 'NWC'), feature_group_count=D_RNN) + conv_b
    rec = _rg_lru(xr, lru_w_x, lru_b_x, lru_w_a, lru_b_a, lru_lambda) \
        * jax.nn.gelu(gr.astype(jnp.float32), approximate=True)
    mixed = jnp.concatenate([attn, rec], axis=-1).astype(h.dtype)
    return mixed @ w_out

def setup_inputs(seed: int = 0) -> dict:
    key = jax.random.key(seed)
    ks = jax.random.split(key, 20)
    f32 = jnp.float32
    nrm = lambda k, shape, fan_in: jax.random.normal(k, shape, f32) * (fan_in ** -0.5)
    u = jax.random.uniform(ks[17], (DEPTH, D_RNN), f32, minval=0.9, maxval=0.999)
    return {
        "x": jax.random.normal(ks[0], (BATCH, SEQ, D_MODEL), f32),
        "c": jax.random.normal(ks[1], (BATCH, D_MODEL), f32),
        "w_ada": 0.5 * nrm(ks[2], (DEPTH, D_MODEL, N_SUBLAYERS * 3 * D_MODEL), D_MODEL),
        "b_ada": 0.01 * jax.random.normal(ks[3], (DEPTH, N_SUBLAYERS * 3 * D_MODEL), f32),
        "norm_gain": 1.0 + 0.05 * jax.random.normal(ks[4], (DEPTH, 2 * N_SUBLAYERS, D_MODEL), f32),
        "ffn1_w_in": nrm(ks[5], (DEPTH, D_MODEL, 2 * D_FF), D_MODEL),
        "ffn1_w_out": nrm(ks[6], (DEPTH, D_FF, D_MODEL), D_FF),
        "mix_w_in": nrm(ks[7], (DEPTH, D_MODEL, D_IN_PROJ), D_MODEL),
        "conv_w": nrm(ks[8], (DEPTH, CONV_WIDTH, D_RNN), CONV_WIDTH),
        "conv_b": 0.01 * jax.random.normal(ks[9], (DEPTH, D_RNN), f32),
        "lru_w_x": nrm(ks[10], (DEPTH, N_LRU_BLOCKS, LRU_BLOCK, LRU_BLOCK), LRU_BLOCK),
        "lru_b_x": 0.01 * jax.random.normal(ks[11], (DEPTH, D_RNN), f32),
        "lru_w_a": nrm(ks[12], (DEPTH, N_LRU_BLOCKS, LRU_BLOCK, LRU_BLOCK), LRU_BLOCK),
        "lru_b_a": 0.01 * jax.random.normal(ks[13], (DEPTH, D_RNN), f32),
        "lru_lambda": jnp.log(u) - jnp.log1p(-u),
        "mix_w_out": nrm(ks[14], (DEPTH, D_MIX, D_MODEL), D_MIX),
        "ffn2_w_in": nrm(ks[15], (DEPTH, D_MODEL, 2 * D_FF), D_MODEL),
        "ffn2_w_out": nrm(ks[16], (DEPTH, D_FF, D_MODEL), D_FF),
    }

def reference(x, c, w_ada, b_ada, norm_gain, ffn1_w_in, ffn1_w_out, mix_w_in, conv_w, conv_b,
              lru_w_x, lru_b_x, lru_w_a, lru_b_a, lru_lambda, mix_w_out, ffn2_w_in, ffn2_w_out):
    f32 = jnp.float32
    B = x.shape[0]
    for l in range(DEPTH):
        mod = jax.nn.silu(c.astype(f32)) @ w_ada[l].astype(f32) + b_ada[l].astype(f32)
        mod = mod.reshape(B, N_SUBLAYERS, 3, D_MODEL)
        shift, scale, gate = mod[:, :, 0], mod[:, :, 1], mod[:, :, 2]
        g = norm_gain[l].astype(f32)

        h = _pre(x, g[0], shift[:, 0], scale[:, 0])
        y = _swiglu(h, ffn1_w_in[l], ffn1_w_out[l])
        x = _post_residual(x, y, g[1], gate[:, 0], FFN_RES_WEIGHT)

        h = _pre(x, g[2], shift[:, 1], scale[:, 1])
        y = _hybrid_mixer(h, mix_w_in[l], conv_w[l], conv_b[l], lru_w_x[l], lru_b_x[l],
                          lru_w_a[l], lru_b_a[l], lru_lambda[l], mix_w_out[l])
        x = _post_residual(x, y, g[3], gate[:, 1], 1.0)

        h = _pre(x, g[4], shift[:, 2], scale[:, 2])
        y = _swiglu(h, ffn2_w_in[l], ffn2_w_out[l])
        x = _post_residual(x, y, g[5], gate[:, 2], FFN_RES_WEIGHT)
    return x


_drawn_inputs = setup_inputs


def setup_inputs(seed=0):
    import zlib

    import numpy as np

    out = dict(_drawn_inputs(seed))
    spreads = {}
    factors = {'conv_b': 3.66, 'lru_b_x': 23.944, 'lru_b_a': 40.567}
    for name, (base, spread) in spreads.items():
        noise = np.random.default_rng([zlib.crc32(name.encode()), seed]).standard_normal(out[name].shape)
        drawn = base * np.exp(spread * noise) if base else spread * noise
        out[name] = __import__('jax').numpy.asarray(drawn.astype(out[name].dtype))
    for name, factor in factors.items():
        out[name] = (out[name] * factor).astype(out[name].dtype)
    return out
```

```python
from contextlib import ExitStack

import numpy as np
import concourse.bass as bass
from concourse import mybir

D, S, FF, P = 1024, 512, 2816, 128
KD, KF = D // P, FF // P
DA = DR = D // 2
HD, HEADS = 64, 8
NT = S // P
CT = DR // P
TAPS = 4
EPS = 1e-6
F32, F32R, I32 = mybir.dt.float32, mybir.dt.float32r, mybir.dt.int32
ALU, ACT = mybir.AluOpType, mybir.ActivationFunctionType
SLOTS = 4

PHASES = [("ffn_in", KF, KD // 2), ("ffn_out", KD // 2, KF // 2), ("mix_in", 10, KD // 2),
          ("mix_out", KD // 2, KD // 2), ("ffn_in", KF, KD // 2), ("ffn_out", KD // 2, KF // 2)]
START = [0]
for _, g_, c_ in PHASES:
    START.append(START[-1] + g_ * c_)
USES = [[0] * SLOTS]
for _, g_, c_ in PHASES:
    USES.append([USES[-1][s] + g_ * len(range(s, c_, SLOTS)) for s in range(SLOTS)])
MIX_ORDER = [0, 2, 4, 1, 3, 5, 6, 7, 8, 9]

ADA_COLS = 9 * D // 512
NU = HEADS * NT


def back(ph, g0, c):
    if PHASES[ph][2] == 4 and not (g0 and ph and PHASES[ph - 1][2] != 4):
        return 4
    if PHASES[ph][2] != 4 and g0:
        return 4
    return 3 if c < 3 else 7 if c == 3 else 4


def locate(n):
    ph = max(i for i in range(6) if START[i] <= n)
    g, c = divmod(n - START[ph], PHASES[ph][2])
    return ph, g, c


def mixer_events():
    ev = {}

    def at(h, *e):
        ev.setdefault(h, []).append(e)

    for gi in range(8):
        at(8 * (gi + 1), "evac", gi)
    at(25, "vtr", 0); at(26, "vtr", 1)
    at(49, "vtr", 2); at(50, "vtr", 3)
    for pair, h in ((0, 57), (1, 65)):
        a, b = 2 * pair, 2 * pair + 1
        at(h, "conv", a); at(h + 1, "conv", b)
        at(h + 2, "gate_x", a); at(h + 3, "gate_a", a)
        at(h + 4, "gate_x", b); at(h + 5, "gate_a", b)
        at(h + 6, "scan", pair)
    at(73, "gelu", 0); at(74, "gelu", 1); at(75, "rec", 0); at(76, "rec", 1)
    at(80, "gelu", 2); at(81, "gelu", 3); at(82, "rec", 2); at(83, "rec", 3)
    for i in range(NU + 2):
        at(27 + (3 * i) // 2, "att", i)
    return ev


EVENTS = mixer_events()


def build(nc, x, c, w_ada, b_ada, norm_gain, ffn1_w_in, ffn1_w_out, mix_w_in, conv_w, conv_b,
          lru_w_x, lru_b_x, lru_w_a, lru_b_a, lru_lambda, mix_w_out, ffn2_w_in, ffn2_w_out, out):
    ctx = ExitStack()
    with ctx:
        def sem(name):
            return ctx.enter_context(nc.semaphore(name))

        place = [-(-nc.sbuf_base // 32) * 32]

        def sb(name, shape, dt=F32, at=None):
            size = int(np.prod(shape[1:])) * 4
            off = place[0] if at is None else at
            if at is None:
                place[0] += -(-size // 32) * 32
            return nc.alloc_sbuf_tensor_at(name, shape, dt, offset=off)

        xT = sb("xT", [P, KD, S])
        h_hi = sb("h_hi", [P, KD, S], F32R)
        h_lo = sb("h_lo", [P, KD, S], F32R)
        y_at = place[0]
        y = sb("y", [P, KD, S])
        arena = place[0]
        hid_hi = sb("hid_hi", [P, KF, S], F32R)
        hid_lo = sb("hid_lo", [P, KF, S], F32R)
        arena_end = place[0]
        raw = sb("raw", [P, SLOTS, 512])
        w_hi = sb("w_hi", [P, SLOTS, 512], F32R)
        w_lo = sb("w_lo", [P, SLOTS, 512], F32R)
        ada_raw = sb("ada_raw", [P, SLOTS, 512])
        ada_acc = sb("ada_acc", [P, 2, 512])
        tmp = sb("tmp", [P, 2, S])
        hid_f = sb("hid_f", [P, S])
        yacc = hid_f
        rstd = sb("rstd", [P, 2, S])
        ones = sb("ones", [P, P])
        ident = sb("ident", [P, P])
        mask = sb("mask", [P, S])
        wx = sb("wx", [P, CT, P])
        wa = sb("wa", [P, CT, P])
        cols_a = sb("cols_a", [P, 120])
        cols_b = sb("cols_b", [P, 40])
        silu_c = sb("silu_c", [P, 3, KD])
        mod = sb("mod", [P, 72])
        A = sb("A", [P, 3, KD])
        G = sb("G", [P, 3, KD])
        eps = sb("eps", [P, 1])
        half_b = sb("half_b", [P, 2, CT])
        sp = sb("sp", [P, 8, CT])
        neg_max = sb("neg_max", [P, 2, 1])
        den = sb("den", [P, 2, 1])
        rden = sb("rden", [P, 2, 1])
        assert place[0] <= nc.sbuf_usable_end, (place[0], nc.sbuf_usable_end)
        x_in = sb("x_in", [P, NT, D], at=y_at)
        vT = sb("vT", [P, 4, S], at=y_at)
        att = sb("att", [P, 2, S], at=y_at + 8192)
        pT = sb("pT", [P, 2, S], at=y_at + 12288)
        qT = sb("qT", [P, 4, S], at=arena)
        kT = sb("kT", [P, 4, S], at=arena + 8192)
        v_nat = sb("v_nat", [P, NT, DA], at=arena + 16384)
        mix_hi = sb("mix_hi", [P, KD, S], F32R, at=arena + 24576)
        mix_lo = sb("mix_lo", [P, KD, S], F32R, at=arena + 40960)
        xr = sb("xr", [P, CT, S + 8], at=arena + 57344)
        gel = sb("gel", [P, CT, S], at=arena + 65664)
        lru = sb("lru", [P, 7, S], at=arena + 73856)
        o_st = sb("o_st", [P, NT, D], at=arena)
        iot = sb("iot", [P, 3, S], I32, at=arena)
        cnt = sb("cnt", [P, 3, S], at=arena + 8192)
        rows_a = sb("rows_a", [120, P], at=arena + 16384)
        rows_b = sb("rows_b", [40, P], at=arena + 16896)
        assert arena + 73856 + 7 * 2048 <= arena_end
        xc = [lru[:, 0, :], lru[:, 1, :]]
        tx = [lru[:, 2, :], lru[:, 3, :]]
        aa = [lru[:, 4, :], lru[:, 5, :]]
        om = [lru[:, 6, :], hid_f[:, :]]

        ps = [ctx.enter_context(nc.psum_tensor(f"ps{i}", [P, 512], F32)) for i in range(8)]
        bank_ss, bank_ys, bank_mod, bank_tr = ps[4], ps[5], ps[6], ps[7]
        bank_s, bank_g, bank_pt, bank_o = ps[4], ps[5], ps[6], ps[7]

        consts_in = sem("consts_in")
        x_loaded = sem("x_loaded")
        wbd_in = sem("wbd_in")
        wbd_zero = sem("wbd_zero")
        out_done = sem("out_done")
        raw_in = [sem(f"raw_in{s}") for s in range(SLOTS)]
        ada_in = [sem(f"ada_in{s}") for s in range(SLOTS)]
        pool_consts = sem("pool_consts")
        pool_iota = sem("pool_iota")
        hi_done = sem("hi_done")
        lo_done = sem("lo_done")
        chunk_used = sem("chunk_used")
        cols_tr = sem("cols_tr")
        cols_ready = sem("cols_ready")
        tanh_c = sem("tanh_c")
        lam_abs = sem("lam_abs")
        silu_c_ready = sem("silu_c_ready")
        ada_done = sem("ada_done")
        ada_col = sem("ada_col")
        mod_ready = sem("mod_ready")
        x_tr = sem("x_tr")
        x0_ready = sem("x0_ready")
        xt_ready = sem("xt_ready")
        sq_ready = sem("sq_ready")
        ss_done = sem("ss_done")
        rms_ready = sem("rms_ready")
        rstd_ready = sem("rstd_ready")
        h_scaled = sem("h_scaled")
        h_hi_done = sem("h_hi_done")
        h_ready = sem("h_ready")
        tanh_done = sem("tanh_done")
        silu_done = sem("silu_done")
        hid_f_done = sem("hid_f_done")
        hid_hi_done = sem("hid_hi_done")
        hid_ready = sem("hid_ready")
        ysq_done = sem("ysq_done")
        y_done = sem("y_done")
        yacc_zero = sem("yacc_zero")
        yacc_done = sem("yacc_done")
        ysum_done = sem("ysum_done")
        t_ready = sem("t_ready")
        out_tr = sem("out_tr")
        out_a = sem("out_a")
        out_v = sem("out_v")
        dve_step = sem("dve_step")
        act_step = sem("act_step")
        mix_evac = sem("mix_evac")
        xr_zero = sem("xr_zero")
        v_tr = sem("v_tr")
        v_ready = sem("v_ready")
        s_done = sem("s_done")
        negs_done = sem("negs_done")
        exp_done = sem("exp_done")
        p_ready = sem("p_ready")
        pt_done = sem("pt_done")
        pt_ready = sem("pt_ready")
        pv_done = sem("pv_done")
        o_hi_done = sem("o_hi_done")
        o_lo_done = sem("o_lo_done")
        conv_done = sem("conv_done")
        gate_done = sem("gate_done")
        tx_done = sem("tx_done")
        lru_a_done = sem("lru_a_done")
        om_done = sem("om_done")
        sqrt_done = sem("sqrt_done")
        scan_done = sem("scan_done")
        gsq_done = sem("gsq_done")
        gu_done = sem("gu_done")
        gt_done = sem("gt_done")
        gel_done = sem("gel_done")
        rec_f_done = sem("rec_f_done")
        rec_hi_done = sem("rec_hi_done")
        rec_ready = sem("rec_ready")

        w_in = {0: ffn1_w_in, 4: ffn2_w_in}
        w_out = {1: ffn1_w_out, 3: mix_w_out, 5: ffn2_w_out}

        def chunk_source(ph, g, c):
            if ph in w_in:
                v = w_in[ph].rearrange("(k p) (u f) -> p k u f", p=P, u=2)
                return [v[:, 2 * c + kk, :, bass.ds(g * P, P)] for kk in range(2)]
            if ph == 2:
                v = mix_w_in.rearrange("(k p) f -> p k f", p=P)
                return [v[:, 2 * c:2 * c + 2, MIX_ORDER[g] * 256:MIX_ORDER[g] * 256 + 256]]
            v = w_out[ph].rearrange("(k p) f -> p k f", p=P)
            return [v[:, 2 * c:2 * c + 2, bass.ds(g * 256, 256)]]

        def filled(ph, g, c):
            s = c % SLOTS
            per_group = len(range(s, PHASES[ph][2], SLOTS))
            dmas = USES[ph][s] + c // SLOTS + 1
            before = sum(2 * (USES[q + 1][s] - USES[q][s]) if q in w_in else USES[q + 1][s] - USES[q][s]
                         for q in range(ph))
            each = 2 if ph in w_in else 1
            return 16 * (before + each * (c // SLOTS + 1)) + 16 * each * per_group * g

        def number(ph, g, c):
            return START[ph] + PHASES[ph][2] * g + c

        block = ctx.enter_context(nc.Block())

        @block.sync
        def _(sp_):
            def load_chunk(ph, g, c, g0):
                n = number(ph, g, c)
                s = c % SLOTS
                b = back(ph, g0, c)
                if not isinstance(n, int) or n - b >= 0:
                    sp_.wait_ge(lo_done, n - b + 1)
                for kk, src in enumerate(chunk_source(ph, g, c)):
                    if ph in w_in:
                        dst = raw[:, s, kk * 256:kk * 256 + 256].rearrange("p (u f) -> p u f", u=2)
                    else:
                        dst = raw[:, s, :].rearrange("p (k f) -> p k f", k=2)
                    sp_.dma_start(dst, src).then_inc(raw_in[s], 16)

            ada_v = w_ada.rearrange("(k p) n -> p k n", p=P)

            def load_ada(col, k, a):
                if not isinstance(a, int) or a >= SLOTS:
                    sp_.wait_ge(ada_done, a - SLOTS + 1)
                sp_.dma_start(ada_raw[:, k % SLOTS, :], ada_v[:, k, bass.ds(col * 512, 512)])\
                    .then_inc(ada_in[k % SLOTS], 16)

            sp_.dma_start(rows_b[0:8, :], c.rearrange("(k p) -> k p", p=P)).then_inc(consts_in, 16)
            for k in range(SLOTS):
                load_ada(0, k, k)
            sp_.dma_start(rows_b[8:24, :], conv_w.rearrange("w (t p) -> (w t) p", p=P)).then_inc(consts_in, 16)
            for i, v in enumerate((conv_b, lru_b_x, lru_b_a, lru_lambda)):
                sp_.dma_start(rows_b[24 + 4 * i:28 + 4 * i, :], v.rearrange("(t p) -> t p", p=P))\
                    .then_inc(consts_in, 16)
            sp_.dma_start(rows_a[0:72, :], b_ada.rearrange("(t p) -> t p", p=P)).then_inc(consts_in, 16)
            sp_.dma_start(rows_a[72:120, :], norm_gain.rearrange("s (t p) -> (s t) p", p=P))\
                .then_inc(consts_in, 16)
            for k in range(SLOTS, KD):
                load_ada(0, k, k)
            for t in range(NT):
                sp_.dma_start(x_in[:, t, :], x[t * P:(t + 1) * P, :]).then_inc(x_loaded, 16)
                load_ada(1, 2 * t, 8 + 2 * t)
                load_ada(1, 2 * t + 1, 9 + 2 * t)
            for col in (2, 3):
                for k in range(KD):
                    load_ada(col, k, 8 * col + k)
                for cc in (0, 1) if col == 2 else (2, 3):
                    load_chunk(0, 0, cc, True)
            sp_.wait_ge(wbd_zero, 1)
            for w, dst in ((lru_w_x, wx), (lru_w_a, wa)):
                v = w.rearrange("(t b) i j -> b i t j", b=2)
                for b in range(2):
                    sp_.dma_start(dst[64 * b:64 * b + 64, :, 64 * b:64 * b + 64], v[b])\
                        .then_inc(wbd_in, 16)
            for g in range(2):
                if g:
                    for cc in range(4):
                        load_chunk(0, 1, cc, False)
                for k in range(KD):
                    load_ada(4 + g, k, 8 * (4 + g) + k)
            with sp_.Fori(1, KF // 2) as i:
                for b in range(2):
                    for cc in range(4):
                        load_chunk(0, 2 * i + b, cc, False)
                    for k in range(4 * b, 4 * b + 4):
                        load_ada(5 + i, k, 40 + 8 * i + k)
            for g in range(4):
                for cc in range(KF // 2):
                    if cc == 4:
                        for k in range(4 * (g % 2), 4 * (g % 2) + 4):
                            load_ada(16 + g // 2, k, 8 * (16 + g // 2) + k)
                    load_chunk(1, g, cc, g == 0)
            for ph in (2, 3):
                for g in range(PHASES[ph][1]):
                    for cc in range(4):
                        load_chunk(ph, g, cc, g == 0)
            for g in range(2):
                for cc in range(4):
                    load_chunk(4, g, cc, g == 0)
            with sp_.Fori(1, KF // 2) as i:
                for b in range(2):
                    for cc in range(4):
                        load_chunk(4, 2 * i + b, cc, False)
            for g in range(4):
                for cc in range(KF // 2):
                    load_chunk(5, g, cc, g == 0)
            for half in range(2):
                for t in range(NT):
                    if t % 2 == 0:
                        sp_.wait_ge(out_a, 2 * half + t // 2 + 1)
                    else:
                        sp_.wait_ge(out_v, 2 * half + t // 2 + 1)
                    sp_.dma_start(out[t * P:(t + 1) * P, half * 512:half * 512 + 512],
                                  o_st[:, t, half * 512:half * 512 + 512]).then_inc(out_done, 16)
            sp_.wait_ge(out_done, 16 * 2 * NT)

        @block.gpsimd
        def _(pool):
            nc.gpsimd.memset(ident[:], 0.0).then_inc(pool_consts, 1)
            pool.wait_ge(pool_consts, 1)
            nc.gpsimd.affine_select(out=ident[:], in_=ident[:], compare_op=ALU.not_equal, fill=1.0,
                                    base=0, pattern=[[-1, P]], channel_multiplier=1)\
                .then_inc(pool_consts, 1)
            nc.gpsimd.memset(ones[:], 1.0).then_inc(pool_consts, 1)
            nc.gpsimd.memset(eps[:], EPS).then_inc(pool_consts, 1)
            nc.gpsimd.iota(iot[:, 0, :], [[-1, S]], base=S - P, channel_multiplier=1)\
                .then_inc(pool_iota, 1)
            nc.gpsimd.memset(wx[:], 0.0)
            nc.gpsimd.memset(wa[:], 0.0).then_inc(wbd_zero, 1)

        @block.tensor
        def _(pe):
            def half_chunk(ph, g, c, kk, moving, done):
                n = number(ph, g, c)
                s = c % SLOTS
                k = 2 * c + kk
                last_k = PHASES[ph][2] * 2 - 1
                hi, lo = moving
                if kk == 0:
                    pe.wait_ge(lo_done, n + 1)
                bank0 = 2 * (g % 2) if isinstance(g, int) else None
                for b in range(2):
                    o = ps[bank0 + b][:, :]
                    col = kk * 256 + b * P
                    wh, wl = w_hi[:, s, col:col + P], w_lo[:, s, col:col + P]
                    nc.tensor.matmul(o, wh, hi, start=(k == 0), stop=False)
                    nc.tensor.matmul(o, wh, lo, start=False, stop=False)
                    last = nc.tensor.matmul(o, wl, hi, start=False, stop=(k == last_k))
                if kk == 1:
                    last.then_inc(chunk_used, 1)

            def in_group(ph, g, parity, first):
                for c in range(KD // 2):
                    n = START[ph] + 4 * g + c
                    pe.wait_ge(lo_done, n + 1)
                    for kk in range(2):
                        k = 2 * c + kk
                        if first:
                            pe.wait_ge(h_ready, 8 * (ph // 2) + k + 1)
                        for b in range(2):
                            o = ps[2 * parity + b][:, :]
                            col = kk * 256 + b * P
                            wh, wl = w_hi[:, c, col:col + P], w_lo[:, c, col:col + P]
                            nc.tensor.matmul(o, wh, h_hi[:, k, :], start=(k == 0), stop=False)
                            nc.tensor.matmul(o, wh, h_lo[:, k, :], start=False, stop=False)
                            last = nc.tensor.matmul(o, wl, h_hi[:, k, :], start=False, stop=(k == KD - 1))
                    last.then_inc(chunk_used, 1)

            def sum_mod(col, a, buf):
                pe.wait_ge(ada_done, a)
                for j in range(4):
                    dst = bank_mod[:, bass.ds(4 * col + j, 1)]
                    last = nc.tensor.matmul(dst, ada_acc[:, buf, j * P:(j + 1) * P], ones[:, 0:1],
                                            start=True, stop=True)
                last.then_inc(ada_col, 1)

            def sum_squares(s):
                for k in range(KD):
                    pe.wait_ge(sq_ready, 8 * s + k + 1)
                    if k == 0 and s:
                        pe.wait_ge(rms_ready, 2 * s)
                    nc.tensor.matmul(bank_ss[:, :], ones[:, :], tmp[:, k % 2, :],
                                     start=(k == 0), stop=(k == KD - 1)).then_inc(ss_done, 1)

            def sum_y(s):
                pe.wait_ge(yacc_done, 8 * (s + 1))
                nc.tensor.matmul(bank_ys[:, :], ones[:, :], yacc[:, :], start=True, stop=True)\
                    .then_inc(ysum_done, 1)

            def ffn(f):
                ph = 4 * f
                for g in range(2):
                    if g == 1 and f == 0:
                        pass
                    in_group(ph, g, g, g == 0)
                    if f == 0:
                        sum_mod(4 + g, 8 * (5 + g), 0)
                with pe.Fori(1, KF // 2) as i:
                    for b in range(2):
                        pe.wait_ge(hid_f_done, KF * f + 2 * i + b - 1)
                        in_group(ph, 2 * i + b, b, False)
                    if f == 0:
                        sum_mod(5 + i, 8 * (6 + i), 0)
                ph += 1
                for g in range(4):
                    if g < 2:
                        pe.wait_ge(hid_f_done, KF * (f + 1) - 1 + g)
                    else:
                        pe.wait_ge(y_done, 16 * f + 2 * (g - 1))

                    def mm(c, slot, start, stop):
                        for kk in range(2):
                            if g == 0 and isinstance(c, int):
                                pe.wait_ge(hid_ready, KF * f + 2 * c + kk + 1)
                            k = 2 * c + kk
                            mh, ml = hid_hi[:, k, :], hid_lo[:, k, :]
                            for b in range(2):
                                o = ps[2 * (g % 2) + b][:, :]
                                col = kk * 256 + b * P
                                wh, wl = w_hi[:, slot, col:col + P], w_lo[:, slot, col:col + P]
                                nc.tensor.matmul(o, wh, mh, start=start and kk == 0, stop=False)
                                nc.tensor.matmul(o, wh, ml, start=False, stop=False)
                                last = nc.tensor.matmul(o, wl, mh, start=False, stop=stop and kk == 1)
                        last.then_inc(chunk_used, 1)

                    for c in range(KF // 2):
                        pe.wait_ge(lo_done, number(ph, g, c) + 1)
                        mm(c, c % SLOTS, c == 0, c == KF // 2 - 1)
                    if f == 0 and g % 2:
                        sum_mod(16 + g // 2, 8 * (17 + g // 2), 0)

            pe.wait_ge(pool_consts, 4)
            pe.wait_ge(consts_in, 16 * 8)
            nc.tensor.transpose(bank_tr[:, 0:120], rows_a[:, :], ident[0:120, 0:120])
            nc.tensor.transpose(bank_tr[:, 128:168], rows_b[:, :], ident[0:40, 0:40]).then_inc(cols_tr, 1)
            pe.wait_ge(x_loaded, 16 * NT)
            for k in range(KD):
                if k >= 4:
                    pe.wait_ge(x0_ready, k - 3)
                for t in range(NT):
                    last = nc.tensor.transpose(ps[k % 4][:, t * P:(t + 1) * P],
                                               x_in[:, t, k * P:(k + 1) * P], ident[:, :])
                last.then_inc(x_tr, 1)
            sum_squares(0)
            for col in range(4):
                sum_mod(col, 8 * (col + 1), col % 2)
            ffn(0)
            sum_y(0)
            sum_squares(1)

            def vtr(t):
                pe.wait_ge(mix_evac, 3 if t < 2 else 6)
                if t:
                    pe.wait_ge(v_ready, t)
                for j in range(NT):
                    last = nc.tensor.transpose(bank_g[:, j * P:(j + 1) * P], vT[:, t, j * P:(j + 1) * P],
                                               ident[:, :])
                last.then_inc(v_tr, 1)

            def att_step(i):
                if i < NU:
                    h, qt = divmod(i, NT)
                    p, r = h // 2, HD * (h % 2)
                    if i:
                        pe.wait_ge(negs_done, i)
                    if h % 4 == 0 and qt == 0:
                        pe.wait_ge(mix_evac, 2 if h == 0 else 5)
                    nc.tensor.matmul(bank_s[:, 0:(qt + 1) * P], qT[r:r + HD, p, qt * P:(qt + 1) * P],
                                     kT[r:r + HD, p, 0:(qt + 1) * P], start=True, stop=True)\
                        .then_inc(s_done, 1)
                if 1 <= i <= NU:
                    u = i - 1
                    qt = u % NT
                    pe.wait_ge(p_ready, u + 1)
                    if u:
                        pe.wait_ge(pt_ready, u)
                    for j in range(qt + 1):
                        last = nc.tensor.transpose(bank_pt[:, j * P:(j + 1) * P],
                                                   att[:, u % 2, j * P:(j + 1) * P], ident[:, :])
                    last.then_inc(pt_done, 1)
                if i >= 2:
                    u = i - 2
                    h, qt = divmod(u, NT)
                    p, r = h // 2, HD * (h % 2)
                    pe.wait_ge(pt_ready, u + 1)
                    if u % 16 == 0:
                        pe.wait_ge(v_ready, 2 if u == 0 else 4)
                    if u and u % 8 == 0:
                        pe.wait_ge(o_lo_done, p)
                    for j in range(qt + 1):
                        last = nc.tensor.matmul(bank_o[r:r + HD, qt * P:(qt + 1) * P],
                                                v_nat[:, j, h * HD:(h + 1) * HD],
                                                pT[:, u % 2, j * P:(j + 1) * P],
                                                start=(j == 0), stop=(j == qt))
                    last.then_inc(pv_done, 1)

            def gate(t, w, n):
                pe.wait_ge(conv_done, t + 1)
                if n == 0:
                    pe.wait_ge(wbd_in, 64)
                    pe.wait_ge(v_ready, 4)
                elif n % 2:
                    pe.wait_ge(tx_done, n // 2 + 1)
                else:
                    pe.wait_ge(lru_a_done, n // 2)
                nc.tensor.matmul(bank_g[:, :], w[:, t, :], xc[t % 2], start=True, stop=True)\
                    .then_inc(gate_done, 1)

            for hp in range(112):
                ph, g, c = locate(START[2] + hp // 2)
                kk = hp % 2
                k = 2 * c + kk
                if ph == 2:
                    if g == 0:
                        pe.wait_ge(h_ready, 8 + k + 1)
                    elif g == 1 and k == 0:
                        pe.wait_ge(y_done, 8)
                    if g >= 2 and k == 0:
                        if g - 2 < 8:
                            pe.wait_ge(mix_evac, g - 1)
                    half_chunk(2, g, c, kk, (h_hi[:, k, :], h_lo[:, k, :]), None)
                else:
                    if g < 2 and k == 0:
                        pe.wait_ge(gel_done, 2 if g == 0 else 4)
                    if g >= 2 and k == 0:
                        pe.wait_ge(y_done, 8 + 2 * (g - 1))
                    if g == 0:
                        if k < 4:
                            pe.wait_ge(o_lo_done, k + 1)
                        else:
                            pe.wait_ge(rec_ready, k - 3)
                    half_chunk(3, g, c, kk, (mix_hi[:, k, :], mix_lo[:, k, :]), None)
                for e, arg in EVENTS.get(hp, ()):
                    if e == "vtr":
                        vtr(arg)
                    elif e == "att":
                        att_step(arg)
                    elif e == "gate_x":
                        gate(arg, wx, 2 * arg)
                    elif e == "gate_a":
                        gate(arg, wa, 2 * arg + 1)
            sum_y(1)
            sum_squares(2)
            ffn(1)
            sum_y(2)
            for k in range(KD):
                pe.wait_ge(xt_ready, 16 + k + 1)
                if k == 0:
                    pe.wait_ge(y_done, 24)
                for t in range(NT):
                    last = nc.tensor.transpose(ps[2 * t + k // 4][:, (k % 4) * P:(k % 4 + 1) * P],
                                               xT[:, k, t * P:(t + 1) * P], ident[:, :])
                last.then_inc(out_tr, 1)

        @block.scalar
        def _(act):
            def cut_hi(ph, g, c, g0):
                n = number(ph, g, c)
                b = back(ph, g0, c)
                act.wait_ge(raw_in[c % SLOTS], filled(ph, g, c))
                if not isinstance(n, int) or n - b >= 0:
                    act.wait_ge(chunk_used, n - b + 1)
                nc.scalar.activation(w_hi[:, c % SLOTS, :], raw[:, c % SLOTS, :], ACT.Copy)\
                    .then_inc(hi_done, 1)

            def cut_hi_n(n):
                if n < START[6]:
                    ph, g, c = locate(n)
                    cut_hi(ph, g, c, g == 0)

            def squares(s, wait):
                for k in range(KD):
                    wait(k)
                    if k >= 2:
                        act.wait_ge(ss_done, 8 * s + k - 1)
                    nc.scalar.activation(tmp[:, k % 2, :], xT[:, k, :], ACT.Square).then_inc(sq_ready, 1)

            def rms(j, bank, wait_sem, value):
                act.wait_ge(wait_sem, value)
                nc.scalar.activation(rstd[:, j % 2, :], bank[:, :], ACT.Sqrt, bias=eps[:, 0:1],
                                     scale=1.0 / D).then_inc(rms_ready, 1)

            def cut_h(s):
                for k in range(KD):
                    act.wait_ge(h_scaled, 8 * s + k + 1)
                    m = 24 * s + k
                    nc.scalar.activation(h_hi[:, k, :], tmp[:, k % 2, :], ACT.Identity,
                                         bias=mod[:, m:m + 1]).then_inc(h_hi_done, 1)

            def swiglu(f, g, parity, first):
                act.wait_ge(chunk_used, START[4 * f] + 4 * g + 4)
                if not first:
                    act.wait_ge(hid_f_done, KF * f + g)
                nc.scalar.activation(tmp[:, 0, :], ps[2 * parity][:, :], ACT.Tanh, scale=0.5)\
                    .then_inc(tanh_done, 1)
                act.wait_ge(hid_f_done, KF * f + g + 1)
                dst = hid_hi[:, g, :] if isinstance(g, int) else hid_hi[:, bass.ds(g, 1), :]
                src = hid_f[:, :] if isinstance(g, int) else hid_f[:, :].rearrange("p (o s) -> p o s", o=1)
                nc.scalar.activation(dst, src, ACT.Copy).then_inc(hid_hi_done, 1)

            def take_y(s, ph, g):
                act.wait_ge(chunk_used, number(ph, g, PHASES[ph][2] - 1) + 1)
                for b in range(2):
                    m = 2 * g + b
                    if m >= 2:
                        act.wait_ge(yacc_done, 8 * s + m - 1)
                    nc.scalar.activation(tmp[:, b, :], ps[2 * (g % 2) + b][:, :], ACT.Square)\
                        .then_inc(ysq_done, 1)
                    nc.scalar.activation(y[:, m, :], ps[2 * (g % 2) + b][:, :], ACT.Copy)\
                        .then_inc(y_done, 1)

            def ffn(f):
                ph = 4 * f
                for cc in range(4):
                    cut_hi(ph, 1, cc, False)
                swiglu(f, 0, 0, f == 0)
                with act.Fori(1, KF // 2) as i:
                    for b in range(2):
                        for cc in range(4):
                            cut_hi(ph, 2 * i + b, cc, False)
                        swiglu(f, 2 * i + b - 1, 1 - b, False)
                ph += 1
                for g in range(4):
                    for cc in range(4):
                        cut_hi(ph, g, cc, g == 0)
                    if g == 0:
                        swiglu(f, KF - 1, 1, False)
                    else:
                        take_y(2 * f, ph, g - 1)
                    for cc in range(4, KF // 2):
                        cut_hi(ph, g, cc, g == 0)
                if f == 0:
                    cut_hi_n(START[2])
                    cut_hi_n(START[2] + 1)
                take_y(2 * f, ph, 3)

            act.wait_ge(cols_ready, 1)
            nc.scalar.activation(silu_c[:, 0, :], cols_b[:, 0:8], ACT.Tanh, scale=0.5).then_inc(tanh_c, 1)
            act.wait_ge(lam_abs, 1)
            nc.scalar.activation(sp[:, 1, :], sp[:, 0, :], ACT.Exp, scale=-1.0).then_inc(tanh_c, 1)
            for k in range(KD):
                act.wait_ge(x_tr, k + 1)
                nc.scalar.activation(xT[:, k, :], ps[k % 4][:, :], ACT.Copy).then_inc(x0_ready, 1)
            squares(0, lambda k: act.wait_ge(x0_ready, k + 1))
            rms(0, bank_ss, ss_done, 8)
            for cc in range(4):
                cut_hi(0, 0, cc, True)
            act.wait_ge(mod_ready, 1)
            cut_h(0)
            ffn(0)

            rms(1, bank_ys, ysum_done, 1)
            cut_hi_n(START[2] + 2)
            cut_hi_n(START[2] + 3)
            squares(1, lambda k: act.wait_ge(xt_ready, k + 1))
            rms(2, bank_ss, ss_done, 16)
            cut_h(1)

            def evac(gi):
                grp = MIX_ORDER[gi]
                act.wait_ge(chunk_used, START[2] + 4 * gi + 4)
                if gi == 0:
                    act.wait_ge(xr_zero, 1)
                for b in range(2):
                    t = 2 * (grp % 2) + b
                    src = ps[2 * (gi % 2) + b][:, :]
                    dst = (qT[:, t, :], kT[:, t, :], vT[:, t, :], xr[:, t, 3:3 + S])[grp // 2]
                    last = nc.scalar.activation(dst, src, ACT.Copy)
                last.then_inc(mix_evac, 1)

            def vtr(t):
                act.wait_ge(v_tr, t + 1)
                nc.scalar.activation(v_nat[:, :, t * P:(t + 1) * P],
                                     bank_g[:, :].rearrange("p (j f) -> p j f", j=NT), ACT.Copy)\
                    .then_inc(v_ready, 1)

            def att_step(i):
                if i < NU:
                    w = (i % NT + 1) * P
                    act.wait_ge(negs_done, i + 1)
                    nc.scalar.activation(att[:, i % 2, 0:w], att[:, i % 2, 0:w], ACT.Exp,
                                         bias=neg_max[:, i % 2, :], scale=-1.0,
                                         accum_out=den[:, i % 2, :]).then_inc(exp_done, 1)
                if 1 <= i <= NU:
                    u = i - 1
                    w = (u % NT + 1) * P
                    act.wait_ge(pt_done, u + 1)
                    if u >= 2:
                        act.wait_ge(pv_done, u - 1)
                    nc.scalar.activation(pT[:, u % 2, 0:w], bank_pt[:, 0:w], ACT.Copy).then_inc(pt_ready, 1)
                if i >= 9 and (i - 9) % 8 == 0:
                    p = (i - 9) // 8
                    act.wait_ge(pv_done, 8 * p + 8)
                    nc.scalar.activation(mix_hi[:, p, :], bank_o[:, :], ACT.Copy).then_inc(o_hi_done, 1)

            def gate_x(t):
                act.wait_ge(gate_done, 2 * t + 1)
                if t >= 2:
                    act.wait_ge(scan_done, t - 1)
                nc.scalar.activation(tx[t % 2], bank_g[:, :], ACT.Tanh, bias=half_b[:, 0, t:t + 1],
                                     scale=0.5).then_inc(tx_done, 1)

            def gate_a(t):
                act.wait_ge(gate_done, 2 * t + 2)
                if t:
                    act.wait_ge(om_done, t)
                else:
                    act.wait_ge(h_ready, 16)
                nc.scalar.activation(tmp[:, 0, :], bank_g[:, :], ACT.Tanh, bias=half_b[:, 1, t:t + 1],
                                     scale=0.5).then_inc(act_step, 1)
                act.wait_ge(act_step, t + 1)
                nc.scalar.activation(tmp[:, 1, :], tmp[:, 0, :], ACT.Tanh, bias=sp[:, 6, t:t + 1],
                                     scale=sp[:, 6, t:t + 1])
                nc.scalar.activation(aa[t % 2], tmp[:, 0, :], ACT.Exp, bias=sp[:, 7, t:t + 1],
                                     scale=sp[:, 7, t:t + 1]).then_inc(lru_a_done, 1)

            def scan(pair):
                act.wait_ge(om_done, 2 * pair + 2)
                for b in range(2):
                    nc.scalar.activation(om[b], om[b], ACT.Sqrt).then_inc(sqrt_done, 1)

            def gelu(t):
                act.wait_ge(chunk_used, START[2] + 4 * (8 + t // 2) + 4)
                bank = ps[2 * (t // 2 % 2) + t % 2]
                if t == 0:
                    act.wait_ge(om_done, 4)
                else:
                    act.wait_ge(gel_done, t)
                nc.scalar.activation(tmp[:, 0, :], bank[:, :], ACT.Square).then_inc(gsq_done, 1)
                act.wait_ge(gu_done, t + 1)
                nc.scalar.activation(tmp[:, 0, :], tmp[:, 0, :], ACT.Tanh,
                                     scale=float(np.sqrt(2 / np.pi))).then_inc(gt_done, 1)

            def rec(t):
                act.wait_ge(rec_f_done, t + 1)
                nc.scalar.activation(mix_hi[:, 4 + t, :], tmp[:, 1, :], ACT.Copy).then_inc(rec_hi_done, 1)

            def run_events(hp):
                for e, arg in EVENTS.get(hp, ()):
                    if e == "evac":
                        evac(arg)
                    elif e == "vtr":
                        vtr(arg)
                    elif e == "att":
                        att_step(arg)
                    elif e == "gate_x":
                        gate_x(arg)
                    elif e == "gate_a":
                        gate_a(arg)
                    elif e == "scan":
                        scan(arg)
                    elif e == "gelu":
                        gelu(arg)
                    elif e == "rec":
                        rec(arg)

            for hp in range(112):
                n = START[2] + hp // 2
                if 2 <= hp and hp % 2 == 0 and n < START[4] - 1:
                    cut_hi_n(n + 3)
                if hp >= 88 and hp % 8 == 0:
                    take_y(1, 3, (hp - 80) // 8 - 1)
                run_events(hp)
            take_y(1, 3, 3)
            cut_hi_n(START[4] + 2)
            cut_hi_n(START[4] + 3)

            rms(3, bank_ys, ysum_done, 2)
            squares(2, lambda k: act.wait_ge(xt_ready, 8 + k + 1))
            rms(4, bank_ss, ss_done, 24)
            cut_h(2)
            ffn(1)
            rms(5, bank_ys, ysum_done, 3)
            for half in range(2):
                for t in (0, 2):
                    act.wait_ge(out_tr, 4 * half + 4)
                    nc.scalar.activation(o_st[:, t, half * 512:half * 512 + 512], ps[2 * t + half][:, :],
                                         ACT.Copy).then_inc(out_a, 1)

        @block.vector
        def _(dve):
            steps = [0]

            def link(ins):
                steps[0] += 1
                ins.then_inc(dve_step, 1)
                dve.wait_ge(dve_step, steps[0])

            def cut_lo(ph, g, c, g0):
                n = number(ph, g, c)
                s = c % SLOTS
                dve.wait_ge(hi_done, n + 1)
                nc.vector.tensor_tensor(w_lo[:, s, :], raw[:, s, :], w_hi[:, s, :].bitcast(F32),
                                        ALU.subtract).then_inc(lo_done, 1)

            def cut_lo_n(n):
                if n < START[6]:
                    ph, g, c = locate(n)
                    cut_lo(ph, g, c, g == 0)

            def ada(col, k, a, buf):
                s = k % SLOTS
                dve.wait_ge(ada_in[s], 16 * 2 * col + 16 * (k // SLOTS + 1))
                acc = ada_acc[:, buf, :]
                if k == 0:
                    if not isinstance(col, int) or col >= 2:
                        back_ = 1 if isinstance(col, int) and col < 4 else 0
                        dve.wait_ge(ada_col, col - back_)
                    nc.vector.tensor_scalar(acc, ada_raw[:, s, :], silu_c[:, 2, 0:1], None, ALU.mult)\
                        .then_inc(ada_done, 1)
                else:
                    dve.wait_ge(ada_done, a)
                    nc.vector.scalar_tensor_tensor(acc, ada_raw[:, s, :], silu_c[:, 2, k:k + 1], acc,
                                                   ALU.mult, ALU.add).then_inc(ada_done, 1)

            def finish_mod(lo, hi, count):
                dve.wait_ge(ada_col, count)
                link(nc.vector.tensor_tensor(mod[:, lo:hi], bank_mod[:, lo:hi], cols_a[:, lo:hi], ALU.add))

            def make_a(s):
                return nc.vector.scalar_tensor_tensor(A[:, s, :], mod[:, 24 * s + 8:24 * s + 16], 1.0,
                                                      cols_a[:, 72 + 16 * s:80 + 16 * s], ALU.add, ALU.mult)

            def make_g(s):
                link(nc.vector.scalar_tensor_tensor(G[:, s, :], mod[:, 24 * s + 16:24 * s + 24], 1.0,
                                                    cols_a[:, 80 + 16 * s:88 + 16 * s], ALU.add, ALU.mult))
                if s != 1:
                    link(nc.vector.tensor_scalar(G[:, s, :], G[:, s, :], 0.5, None, ALU.mult))

            def inverse_rms(j):
                dve.wait_ge(rms_ready, j + 1)
                nc.vector.reciprocal(rstd[:, j % 2, :], rstd[:, j % 2, :]).then_inc(rstd_ready, 1)
                dve.wait_ge(rstd_ready, j + 1)

            def cut_h(s):
                for k in range(KD + 1):
                    if k < KD:
                        if k >= 2:
                            dve.wait_ge(h_ready, 8 * s + k - 1)
                        nc.vector.scalar_tensor_tensor(tmp[:, k % 2, :], xT[:, k, :], A[:, s, k:k + 1],
                                                       rstd[:, 0, :], ALU.mult, ALU.mult)\
                            .then_inc(h_scaled, 1)
                    if k:
                        j = k - 1
                        dve.wait_ge(h_hi_done, 8 * s + j + 1)
                        m = 24 * s + j
                        nc.vector.scalar_tensor_tensor(h_lo[:, j, :], tmp[:, j % 2, :], mod[:, m:m + 1],
                                                       h_hi[:, j, :].bitcast(F32), ALU.add,
                                                       ALU.subtract).then_inc(h_ready, 1)

            def residual(s):
                inverse_rms(2 * s + 1)
                for k in range(KD + 1):
                    if k < KD:
                        nc.vector.scalar_tensor_tensor(y[:, k, :], y[:, k, :], G[:, s, k:k + 1],
                                                       rstd[:, 1, :], ALU.mult, ALU.mult)\
                            .then_inc(t_ready, 1)
                    if k:
                        dve.wait_ge(t_ready, 8 * s + k)
                        nc.vector.tensor_tensor(xT[:, k - 1, :], xT[:, k - 1, :], y[:, k - 1, :], ALU.add)\
                            .then_inc(xt_ready, 1)

            def silu_up(f, g, parity):
                dve.wait_ge(tanh_done, KF * f + g + 1)
                nc.vector.scalar_tensor_tensor(tmp[:, 1, :], tmp[:, 0, :], 1.0, ps[2 * parity][:, :],
                                               ALU.add, ALU.mult).then_inc(silu_done, 1)
                dve.wait_ge(silu_done, KF * f + g + 1)
                if not isinstance(g, int) or g:
                    dve.wait_ge(hid_ready, KF * f + g)
                nc.vector.scalar_tensor_tensor(hid_f[:, :], tmp[:, 1, :], 0.5, ps[2 * parity + 1][:, :],
                                               ALU.mult, ALU.mult).then_inc(hid_f_done, 1)

            def cut_hid(f, g):
                dve.wait_ge(hid_hi_done, KF * f + g + 1)
                if isinstance(g, int):
                    o, i0, i1 = hid_lo[:, g, :], hid_f[:, :], hid_hi[:, g, :].bitcast(F32)
                else:
                    o, i1 = hid_lo[:, bass.ds(g, 1), :], hid_hi[:, bass.ds(g, 1), :].bitcast(F32)
                    i0 = hid_f[:, :].rearrange("p (o s) -> p o s", o=1)
                nc.vector.tensor_tensor(o, i0, i1, ALU.subtract).then_inc(hid_ready, 1)

            def zero_yacc(hid_tiles):
                dve.wait_ge(hid_ready, hid_tiles)
                nc.vector.memset(yacc[:, :], 0.0).then_inc(yacc_zero, 1)

            def add_y(s, g):
                for b in range(2):
                    m = 2 * g + b
                    dve.wait_ge(ysq_done, 8 * s + m + 1)
                    if m == 0:
                        dve.wait_ge(yacc_zero, s + 1)
                    else:
                        dve.wait_ge(yacc_done, 8 * s + m)
                    nc.vector.tensor_tensor(yacc[:, :], yacc[:, :], tmp[:, b, :], ALU.add)\
                        .then_inc(yacc_done, 1)

            def ffn(f):
                ph = 4 * f
                for cc in range(4):
                    cut_lo(ph, 1, cc, False)
                if f == 0:
                    for k in range(KD):
                        ada(5, k, 40 + k, 0)
                silu_up(f, 0, 0)
                cut_hid(f, 0)
                with dve.Fori(1, KF // 2) as i:
                    for b in range(2):
                        for cc in range(4):
                            cut_lo(ph, 2 * i + b, cc, False)
                        if f == 0:
                            for k in (4 * b, 4 * b + 1):
                                ada(5 + i, k, 40 + 8 * i + k, 0)
                        silu_up(f, 2 * i + b - 1, 1 - b)
                        if f == 0:
                            for k in (4 * b + 2, 4 * b + 3):
                                ada(5 + i, k, 40 + 8 * i + k, 0)
                        cut_hid(f, 2 * i + b - 1)
                ph += 1
                for g in range(4):
                    for cc in range(4):
                        cut_lo(ph, g, cc, g == 0)
                    if g == 0:
                        silu_up(f, KF - 1, 1)
                        cut_hid(f, KF - 1)
                        zero_yacc(KF * (f + 1))
                        if f == 0:
                            finish_mod(16, 64, 16)
                            for s in (0, 1):
                                make_g(s)
                            link(make_a(1))
                    else:
                        add_y(2 * f, g - 1)
                    for cc in range(4, KF // 2):
                        cut_lo(ph, g, cc, g == 0)
                        if f == 0 and cc < 8:
                            kk = 4 * (g % 2) + cc - 4
                            ada(16 + g // 2, kk, 8 * (16 + g // 2) + kk, 0)
                if f == 0:
                    cut_lo_n(START[2])
                    cut_lo_n(START[2] + 1)
                add_y(2 * f, 3)

            dve.wait_ge(cols_tr, 1)
            link(nc.vector.tensor_copy(cols_b[:, :], bank_tr[:, 128:168]))
            nc.vector.tensor_copy(cols_a[:, :], bank_tr[:, 0:120]).then_inc(cols_ready, 1)
            lam = cols_b[:, 36:40]
            link(nc.vector.tensor_scalar(sp[:, 2, :], lam, -1.0, None, ALU.mult))
            nc.vector.tensor_tensor(sp[:, 0, :], sp[:, 2, :], lam, ALU.max).then_inc(lam_abs, 1)
            dve.wait_ge(tanh_c, 1)
            link(nc.vector.scalar_tensor_tensor(silu_c[:, 1, :], silu_c[:, 0, :], 1.0, cols_b[:, 0:8],
                                                ALU.add, ALU.mult))
            link(nc.vector.tensor_scalar(silu_c[:, 2, :], silu_c[:, 1, :], 0.5, None, ALU.mult))
            for col in range(4):
                for k in range(KD):
                    ada(col, k, 8 * col + k, col % 2)
            dve.wait_ge(tanh_c, 2)
            link(nc.vector.tensor_scalar(sp[:, 3, :], sp[:, 1, :], 2.0, None, ALU.add))
            link(nc.vector.reciprocal(sp[:, 3, :], sp[:, 3, :]))
            link(nc.vector.tensor_tensor(sp[:, 3, :], sp[:, 3, :], sp[:, 1, :], ALU.mult))
            link(nc.vector.tensor_tensor(sp[:, 4, :], sp[:, 3, :], sp[:, 3, :], ALU.mult))
            link(nc.vector.memset(sp[:, 5, :], 1.0 / 17))
            for n in (15, 13, 11, 9, 7, 5, 3, 1):
                link(nc.vector.tensor_tensor(sp[:, 5, :], sp[:, 5, :], sp[:, 4, :], ALU.mult))
                link(nc.vector.tensor_scalar(sp[:, 5, :], sp[:, 5, :], 1.0 / n, None, ALU.add))
            link(nc.vector.tensor_tensor(sp[:, 5, :], sp[:, 5, :], sp[:, 3, :], ALU.mult))
            link(nc.vector.tensor_scalar(sp[:, 2, :], sp[:, 2, :], 0.0, 0.5, ALU.max, ALU.mult))
            link(nc.vector.tensor_tensor(sp[:, 5, :], sp[:, 5, :], sp[:, 2, :], ALU.add))
            link(nc.vector.tensor_scalar(sp[:, 6, :], sp[:, 5, :], 8.0, None, ALU.mult))
            link(nc.vector.tensor_scalar(sp[:, 7, :], sp[:, 5, :], -8.0, None, ALU.mult))
            link(nc.vector.tensor_scalar(half_b[:, 0, :], cols_b[:, 28:32], 0.5, None, ALU.mult))
            link(nc.vector.tensor_scalar(half_b[:, 1, :], cols_b[:, 32:36], 0.5, None, ALU.mult))
            finish_mod(0, 16, 4)
            make_a(0).then_inc(mod_ready, 1)
            dve.wait_ge(mod_ready, 1)
            for cc in range(4):
                cut_lo(0, 0, cc, True)
            inverse_rms(0)
            cut_h(0)
            dve.wait_ge(pool_iota, 1)
            for n, bits in ((1, 3), (2, 15)):
                link(nc.vector.tensor_scalar(iot[:, n, :], iot[:, 0, :], bits, None, ALU.bitwise_and))
            link(nc.vector.tensor_copy(cnt[:, 0, :], iot[:, 0, :]))
            link(nc.vector.tensor_scalar(cnt[:, 1, :], cnt[:, 0, :], 128.0, None, ALU.is_le))
            for n in (1, 2):
                link(nc.vector.tensor_copy(cnt[:, 2, :], iot[:, n, :]))
                link(nc.vector.scalar_tensor_tensor(cnt[:, 1, :], cnt[:, 2, :], 0.0, cnt[:, 1, :],
                                                    ALU.is_equal, ALU.add))
            link(nc.vector.scalar_tensor_tensor(cnt[:, 1, :], cnt[:, 0, :], 0.0, cnt[:, 1, :],
                                                ALU.is_ge, ALU.mult))
            link(nc.vector.tensor_scalar(mask[:, :], cnt[:, 1, :], 0.0, -8e30, ALU.is_equal, ALU.mult))
            for n in (2, 3):
                link(nc.vector.tensor_scalar(cnt[:, 2, :], cnt[:, 1, :], float(n), float(8 * np.log(n)),
                                             ALU.is_equal, ALU.mult))
                link(nc.vector.tensor_tensor(mask[:, :], mask[:, :], cnt[:, 2, :], ALU.add))
            for k in range(KD):
                ada(4, k, 32 + k, 0)
            ffn(0)

            cut_lo_n(START[2] + 2)
            cut_lo_n(START[2] + 3)
            residual(0)
            inverse_rms(2)
            cut_h(1)
            finish_mod(64, 72, 18)
            link(make_a(2))
            make_g(2)
            for t in range(CT):
                last = nc.vector.memset(xr[:, t, 0:3], 0.0)
            last.then_inc(xr_zero, 1)

            def att_step(i):
                if 1 <= i <= NU:
                    u = i - 1
                    w = (u % NT + 1) * P
                    dve.wait_ge(exp_done, u + 1)
                    link(nc.vector.reciprocal(rden[:, u % 2, :], den[:, u % 2, :]))
                    nc.vector.tensor_scalar(att[:, u % 2, 0:w], att[:, u % 2, 0:w], rden[:, u % 2, :],
                                            None, ALU.mult).then_inc(p_ready, 1)
                if i < NU:
                    qt = i % NT
                    w = (qt + 1) * P
                    dve.wait_ge(s_done, i + 1)
                    if i >= 2:
                        dve.wait_ge(pt_done, i - 1)
                    nc.vector.tensor_tensor_reduce(out=att[:, i % 2, 0:w], in0=bank_s[:, 0:w],
                                                   in1=mask[:, S - w:S], scale=-1.0 / 8, scalar=3e38,
                                                   op0=ALU.add, op1=ALU.min,
                                                   accum_out=neg_max[:, i % 2, :]).then_inc(negs_done, 1)
                if i >= 9 and (i - 9) % 8 == 0:
                    p = (i - 9) // 8
                    dve.wait_ge(o_hi_done, p + 1)
                    nc.vector.tensor_tensor(mix_lo[:, p, :], bank_o[:, :], mix_hi[:, p, :].bitcast(F32),
                                            ALU.subtract).then_inc(o_lo_done, 1)

            def conv(t):
                dve.wait_ge(mix_evac, 7 + t // 2)
                if t >= 2:
                    dve.wait_ge(gate_done, 2 * t - 2)
                w = 8 + t
                link(nc.vector.tensor_scalar(xc[t % 2], xr[:, t, 0:S], cols_b[:, w:w + 1],
                                             cols_b[:, 24 + t:25 + t], ALU.mult, ALU.add))
                for tap in range(1, TAPS):
                    w += CT
                    last = nc.vector.scalar_tensor_tensor(xc[t % 2], xr[:, t, tap:tap + S],
                                                          cols_b[:, w:w + 1], xc[t % 2], ALU.mult, ALU.add)
                    if tap < TAPS - 1:
                        link(last)
                last.then_inc(conv_done, 1)

            def gate_a(t):
                dve.wait_ge(lru_a_done, t + 1)
                if t >= 2:
                    pass
                link(nc.vector.tensor_tensor(om[t % 2], aa[t % 2], aa[t % 2], ALU.mult))
                nc.vector.scalar_tensor_tensor(om[t % 2], om[t % 2], 1.0, tmp[:, 1, :], ALU.add,
                                               ALU.mult).then_inc(om_done, 1)

            def scan(pair):
                for b in range(2):
                    t = 2 * pair + b
                    dve.wait_ge(tx_done, t + 1)
                    dve.wait_ge(conv_done, t + 1)
                    link(nc.vector.scalar_tensor_tensor(tx[b], tx[b], 1.0, xc[b], ALU.add, ALU.mult))
                    dve.wait_ge(sqrt_done, t + 1)
                    link(nc.vector.scalar_tensor_tensor(tx[b], tx[b], 0.5, om[b], ALU.mult, ALU.mult))
                    nc.vector.tensor_tensor_scan(xr[:, t, 3:3 + S], aa[b], tx[b], 0.0, ALU.mult,
                                                 ALU.add).then_inc(scan_done, 1)

            def gelu(t):
                bank = ps[2 * (t // 2 % 2) + t % 2]
                dve.wait_ge(gsq_done, t + 1)
                link(nc.vector.tensor_scalar(tmp[:, 0, :], tmp[:, 0, :], 0.044715, 1.0, ALU.mult, ALU.add))
                nc.vector.tensor_tensor(tmp[:, 0, :], tmp[:, 0, :], bank[:, :], ALU.mult).then_inc(gu_done, 1)
                dve.wait_ge(gt_done, t + 1)
                nc.vector.scalar_tensor_tensor(gel[:, t, :], tmp[:, 0, :], 1.0, bank[:, :], ALU.add,
                                               ALU.mult).then_inc(gel_done, 1)

            def rec(t):
                dve.wait_ge(gel_done, t + 1)
                dve.wait_ge(scan_done, t + 1)
                if t:
                    dve.wait_ge(rec_ready, t)
                nc.vector.scalar_tensor_tensor(tmp[:, 1, :], xr[:, t, 3:3 + S], 0.5, gel[:, t, :],
                                               ALU.mult, ALU.mult).then_inc(rec_f_done, 1)
                dve.wait_ge(rec_hi_done, t + 1)
                nc.vector.tensor_tensor(mix_lo[:, 4 + t, :], tmp[:, 1, :], mix_hi[:, 4 + t, :].bitcast(F32),
                                        ALU.subtract).then_inc(rec_ready, 1)

            for hp in range(112):
                n = START[2] + hp // 2
                if 2 <= hp and hp % 2 == 0 and n < START[4] - 1:
                    cut_lo_n(n + 3)
                if hp == 80:
                    dve.wait_ge(scan_done, 4)
                    zero_yacc(KF)
                if hp >= 88 and hp % 8 == 0:
                    add_y(1, (hp - 80) // 8 - 1)
                for e, arg in EVENTS.get(hp, ()):
                    if e == "att":
                        att_step(arg)
                    elif e == "conv":
                        conv(arg)
                    elif e == "gate_a":
                        gate_a(arg)
                    elif e == "scan":
                        scan(arg)
                    elif e == "gelu":
                        gelu(arg)
                    elif e == "rec":
                        rec(arg)
            add_y(1, 3)
            cut_lo_n(START[4] + 2)
            cut_lo_n(START[4] + 3)
            residual(1)
            inverse_rms(4)
            cut_h(2)
            ffn(1)
            residual(2)
            for half in range(2):
                for t in (1, 3):
                    dve.wait_ge(out_tr, 4 * half + 4)
                    nc.vector.tensor_copy(o_st[:, t, half * 512:half * 512 + 512], ps[2 * t + half][:, :])\
                        .then_inc(out_v, 1)


_INS = ["x", "c", "w_ada", "b_ada", "norm_gain", "ffn1_w_in", "ffn1_w_out", "mix_w_in", "conv_w", "conv_b",
        "lru_w_x", "lru_b_x", "lru_w_a", "lru_b_a", "lru_lambda", "mix_w_out", "ffn2_w_in", "ffn2_w_out"]


def kernel(**inputs):
    import numpy as _np
    import concourse.bacc as _bacc
    from concourse import mybir as _mybir
    from concourse.bass_utils import run_bass_kernel_spmd as _run

    nc = _bacc.Bacc("TRN2", target_bir_lowering=False, num_devices=1)
    arrays, args = {}, []
    for name in _INS:
        a = _np.ascontiguousarray(inputs[name])
        arrays[f"in_{name}"] = a
        ap = nc.dram_tensor(f"in_{name}", a.shape, _mybir.dt.from_np(a.dtype), kind="ExternalInput").ap()
        args.append(ap[0])
    out = nc.dram_tensor("out_y", (1, S, D), _mybir.dt.float32, kind="ExternalOutput").ap()
    build(nc, *args, out[0])
    r = _run(nc, [arrays], core_ids=[0])
    return r.results[0]["out_y"]
```

```python
from contextlib import ExitStack

import numpy as np
import concourse.bass as bass
from concourse import mybir

D, S, FF, P = 1024, 512, 2816, 128
KD, KF = D // P, FF // P
DA = DR = D // 2
HD, HEADS = 64, 8
NT = S // P
CT = DR // P
TAPS = 4
EPS = 1e-6
F32, F32R, I32 = mybir.dt.float32, mybir.dt.float32r, mybir.dt.int32
ALU, ACT = mybir.AluOpType, mybir.ActivationFunctionType
SLOTS = 4

PHASES = [("ffn_in", KF, KD // 2), ("ffn_out", KD // 2, KF // 2), ("mix_in", 10, KD // 2),
          ("mix_out", KD // 2, KD // 2), ("ffn_in", KF, KD // 2), ("ffn_out", KD // 2, KF // 2)]
START = [0]
for _, g_, c_ in PHASES:
    START.append(START[-1] + g_ * c_)
USES = [[0] * SLOTS]
for _, g_, c_ in PHASES:
    USES.append([USES[-1][s] + g_ * len(range(s, c_, SLOTS)) for s in range(SLOTS)])
MIX_ORDER = [0, 2, 4, 6, 1, 3, 7, 5, 8, 9]
AT = {g: i for i, g in enumerate(MIX_ORDER)}
OUT_ORDER = [2, 0, 1, 3]
ADA_PE = 3
T_LAG, PV_LAG = 2, 4

ADA_COLS = 9 * D // 512
NU = HEADS * NT


def back(ph, j):
    return (3, 3, 3, 7)[j] if j < 4 else 4


def locate(n):
    ph = max(i for i in range(6) if START[i] <= n)
    j = n - START[ph]
    g, c = divmod(j, PHASES[ph][2])
    slot = c % SLOTS
    behind_long = PHASES[ph][2] != 4 and g or PHASES[ph][2] == 4 and g == 0 and ph and PHASES[ph - 1][2] != 4
    b = back(ph, c) if behind_long else 4
    if ph in (0, 2, 4) and j < 8:
        g, c = j % 2, j // 2
    elif ph == 3:
        c = OUT_ORDER[c]
    return ph, g, c, slot, b


def mixer_events():
    ev = {}

    def at(h, *e):
        ev.setdefault(h, []).append(e)

    at(14, "evac", 0)
    for gi in range(1, 10):
        if MIX_ORDER[gi] < 8:
            at(8 * (gi + 1), "evac", gi)
    for half in range(2):
        h = 8 * (AT[4 + half] + 1)
        at(h + 1 + half, "vtr", 2 * half)
        at(h + 2 + half, "vtr", 2 * half + 1)
        a, b = 2 * half, 2 * half + 1
        h = 8 * (AT[6 + half] + 1)
        at(h + 1, "conv", a)
        at(h + 3, "conv", b)
        at(h + 4, "gate_x", a)
        at(h + 6, "gate_a", a)
        at(h + 7, "gate_x", b)
        at(h + 8, "gate_a", b)
        at(h + 11, "scan", half)
        h = 8 * (AT[8 + half] + 1)
        at(h + (1 - half), "gelu", a)
        at(h + 2 - half, "gelu", b)
        at(h + 3 - half, "rec", a)
        at(h + 5 - 2 * half, "rec", b)
    first, second, v2 = 8 * (AT[4] + 1) + 3, 8 * (AT[3] + 1) + 1, 8 * (AT[5] + 1) + 4
    for i in range(NU + PV_LAG):
        if i < 16 + PV_LAG:
            h = first + i * (v2 - first) // (16 + PV_LAG)
            if i >= 16:
                h = max(h, second)
        else:
            h = v2 + i - 16 - PV_LAG
        at(h, "att", i)
    return ev


EVENTS = mixer_events()


def build(nc, x, c, w_ada, b_ada, norm_gain, ffn1_w_in, ffn1_w_out, mix_w_in, conv_w, conv_b,
          lru_w_x, lru_b_x, lru_w_a, lru_b_a, lru_lambda, mix_w_out, ffn2_w_in, ffn2_w_out, out):
    ctx = ExitStack()
    with ctx:
        def sem(name):
            return ctx.enter_context(nc.semaphore(name))

        place = [-(-nc.sbuf_base // 32) * 32]

        def sb(name, shape, dt=F32, at=None):
            size = int(np.prod(shape[1:])) * 4
            off = place[0] if at is None else at
            if at is None:
                place[0] += -(-size // 32) * 32
            return nc.alloc_sbuf_tensor_at(name, shape, dt, offset=off)

        xT = sb("xT", [P, KD, S])
        h_hi = sb("h_hi", [P, KD, S], F32R)
        h_lo = sb("h_lo", [P, KD, S], F32R)
        y_at = place[0]
        y = sb("y", [P, KD, S])
        arena = place[0]
        hid_hi = sb("hid_hi", [P, KF, S], F32R)
        hid_lo = sb("hid_lo", [P, KF, S], F32R)
        arena_end = place[0]
        raw = sb("raw", [P, SLOTS, 512])
        w_hi = sb("w_hi", [P, SLOTS, 512], F32R)
        w_lo = sb("w_lo", [P, SLOTS, 512], F32R)
        ada_raw = sb("ada_raw", [P, SLOTS, 512])
        ada_acc = sb("ada_acc", [P, 2, 512])
        tmp = sb("tmp", [P, 3, S])
        hid_f = sb("hid_f", [P, S])
        yacc = hid_f
        diag = sb("diag", [P, NT, P])
        rms = sb("rms", [P, 2, NT])
        x_ss = sb("x_ss", [P, NT])
        ones = sb("ones", [P, P])
        ident = sb("ident", [P, P])
        mask = sb("mask", [P, S])
        wx = sb("wx", [P, CT, P])
        wa = sb("wa", [P, CT, P])
        cols_a = sb("cols_a", [P, 120])
        cols_b = sb("cols_b", [P, 40])
        silu_c = sb("silu_c", [P, 3, KD])
        mod = sb("mod", [P, 72])
        A = sb("A", [P, 3, KD])
        G = sb("G", [P, 3, KD])
        eps = sb("eps", [P, 1])
        half_b = sb("half_b", [P, 2, CT])
        sp = sb("sp", [P, 8, CT])
        neg_max = sb("neg_max", [P, 4, 1])
        den = sb("den", [P, 4, 1])
        rden = sb("rden", [P, 4, 1])
        assert place[0] <= nc.sbuf_usable_end, (place[0], nc.sbuf_usable_end)
        x_in = sb("x_in", [P, NT, D], at=y_at)
        att = sb("att", [P, 4, S], at=y_at)
        pT = sb("pT", [P, 4, S], at=y_at + 8192)
        qT = sb("qT", [P, 4, S], at=arena)
        kT = sb("kT", [P, 4, S], at=arena + 8192)
        v_nat = sb("v_nat", [P, NT, DA], at=arena + 16384)
        mix_hi = sb("mix_hi", [P, KD, S], F32R, at=arena + 24576)
        mix_lo = sb("mix_lo", [P, KD, S], F32R, at=arena + 40960)
        xr = sb("xr", [P, CT, S + 8], at=arena + 57344)
        gel = sb("gel", [P, CT, S], at=arena + 65664)
        lru = sb("lru", [P, 7, S], at=arena + 73856)
        vT = sb("vT", [P, 2, S], at=arena + 65664)
        o_st = sb("o_st", [P, NT, D], at=arena)
        ada0 = sb("ada0", [P, 4, KD, 512], at=arena)
        iot = sb("iot", [P, 3, S], I32, at=arena + 65536)
        cnt = sb("cnt", [P, 3, S], at=arena + 71680)
        rows_a = sb("rows_a", [120, P], at=arena + 77824)
        rows_b = sb("rows_b", [32, P], at=arena + 78336)
        rows_c = sb("rows_c", [KD, P], at=arena + 78848)
        assert arena + 73856 + 7 * 2048 <= arena_end
        xc = [lru[:, 0, :], lru[:, 1, :]]
        tx = [lru[:, 2, :], lru[:, 3, :]]
        aa = [lru[:, 4, :], lru[:, 5, :]]
        om = [lru[:, 6, :], hid_f[:, :]]

        ps = [ctx.enter_context(nc.psum_tensor(f"ps{i}", [P, 512], F32)) for i in range(8)]
        bank_stat, bank_r, bank_mod, bank_tr = ps[4], ps[5], ps[6], ps[7]
        bank_s, bank_g, bank_pt, bank_o = ps[4], ps[5], ps[6], ps[7]

        consts_in = sem("consts_in")
        c_in = sem("c_in")
        x_loaded = [sem(f"x_loaded{t}") for t in range(NT)]
        ada0_in = [[sem(f"ada0_in{q}_{j}") for j in range(4)] for q in range(4)]
        ada0_done = sem("ada0_done")
        mod0_sum = sem("mod0_sum")
        mod0_ready = sem("mod0_ready")
        c_tr = sem("c_tr")
        c_ready = sem("c_ready")
        diag_ready = sem("diag_ready")
        wbd_in = sem("wbd_in")
        wbd_zero = sem("wbd_zero")
        out_done = sem("out_done")
        raw_in = [sem(f"raw_in{s}") for s in range(SLOTS)]
        ada_in = [sem(f"ada_in{s}") for s in range(SLOTS)]
        pool_consts = sem("pool_consts")
        pool_iota = sem("pool_iota")
        hi_done = sem("hi_done")
        lo_done = sem("lo_done")
        chunk_used = sem("chunk_used")
        cols_tr = sem("cols_tr")
        cols_ready = sem("cols_ready")
        tanh_c = sem("tanh_c")
        lam_abs = sem("lam_abs")
        silu_c_ready = sem("silu_c_ready")
        ada_done = sem("ada_done")
        ada_col = sem("ada_col")
        x_summed = sem("x_summed")
        x_tr = sem("x_tr")
        x0_ready = sem("x0_ready")
        xt_ready = sem("xt_ready")
        sq_ready = sem("sq_ready")
        ss_done = sem("ss_done")
        rms_ready = sem("rms_ready")
        rstd_ready = sem("rstd_ready")
        h_scaled = sem("h_scaled")
        h_hi_done = sem("h_hi_done")
        h_ready = sem("h_ready")
        tanh_done = sem("tanh_done")
        silu_done = sem("silu_done")
        hid_f_done = sem("hid_f_done")
        hid_hi_done = sem("hid_hi_done")
        hid_ready = sem("hid_ready")
        ysq_done = sem("ysq_done")
        y_done = sem("y_done")
        yacc_zero = sem("yacc_zero")
        yacc_done = sem("yacc_done")
        ysum_done = sem("ysum_done")
        t_ready = sem("t_ready")
        out_tr = sem("out_tr")
        out_a = sem("out_a")
        out_v = sem("out_v")
        dve_step = sem("dve_step")
        act_step = sem("act_step")
        mix_evac = sem("mix_evac")
        xr_zero = sem("xr_zero")
        v_tr = sem("v_tr")
        v_ready = sem("v_ready")
        s_done = sem("s_done")
        negs_done = sem("negs_done")
        exp_done = sem("exp_done")
        p_ready = sem("p_ready")
        pt_done = sem("pt_done")
        pt_ready = sem("pt_ready")
        pv_done = sem("pv_done")
        o_hi_done = sem("o_hi_done")
        o_lo_done = sem("o_lo_done")
        conv_done = sem("conv_done")
        gate_done = sem("gate_done")
        tx_done = sem("tx_done")
        lru_a_done = sem("lru_a_done")
        om_done = sem("om_done")
        sqrt_done = sem("sqrt_done")
        scan_done = sem("scan_done")
        gsq_done = sem("gsq_done")
        gu_done = sem("gu_done")
        gt_done = sem("gt_done")
        gel_done = sem("gel_done")
        rec_f_done = sem("rec_f_done")
        rec_hi_done = sem("rec_hi_done")
        rec_ready = sem("rec_ready")

        w_in = {0: ffn1_w_in, 4: ffn2_w_in}
        w_out = {1: ffn1_w_out, 3: mix_w_out, 5: ffn2_w_out}

        def chunk_source(ph, g, c):
            if ph in w_in:
                v = w_in[ph].rearrange("(k p) (u f) -> p k u f", p=P, u=2)
                return [v[:, 2 * c + kk, :, bass.ds(g * P, P)] for kk in range(2)]
            if ph == 2:
                v = mix_w_in.rearrange("(k p) f -> p k f", p=P)
                return [v[:, 2 * c:2 * c + 2, MIX_ORDER[g] * 256:MIX_ORDER[g] * 256 + 256]]
            v = w_out[ph].rearrange("(k p) f -> p k f", p=P)
            return [v[:, 2 * c:2 * c + 2, bass.ds(g * 256, 256)]]

        def filled(ph, g, c):
            s = c % SLOTS
            per_group = len(range(s, PHASES[ph][2], SLOTS))
            before = sum(2 * (USES[q + 1][s] - USES[q][s]) if q in w_in else USES[q + 1][s] - USES[q][s]
                         for q in range(ph))
            each = 2 if ph in w_in else 1
            return 16 * (before + each * (c // SLOTS + 1)) + 16 * each * per_group * g

        def number(ph, g, c):
            return START[ph] + PHASES[ph][2] * g + c

        block = ctx.enter_context(nc.Block())

        @block.sync
        def _(sp_):
            def load(ph, g, c, s, n, b):
                if not isinstance(n, int) or n - b >= 0:
                    sp_.wait_ge(lo_done, n - b + 1)
                for kk, src in enumerate(chunk_source(ph, g, c)):
                    if ph in w_in:
                        dst = raw[:, s, kk * 256:kk * 256 + 256].rearrange("p (u f) -> p u f", u=2)
                    else:
                        dst = raw[:, s, :].rearrange("p (k f) -> p k f", k=2)
                    sp_.dma_start(dst, src).then_inc(raw_in[s], 16)

            def load_n(n):
                ph, g, c, s, b = locate(n)
                load(ph, g, c, s, n, b)

            def load_group(ph, g):
                for c in range(4):
                    load(ph, g, c, c, number(ph, g, c), 4)

            ada_v = w_ada.rearrange("(k p) n -> p k n", p=P)

            def load_ada(col, k, a):
                if not isinstance(a, int) or a >= SLOTS:
                    sp_.wait_ge(ada_done, a - (SLOTS - 1))
                sp_.dma_start(ada_raw[:, k % SLOTS, :], ada_v[:, k, bass.ds(col * 512, 512)])\
                    .then_inc(ada_in[k % SLOTS], 16)

            sp_.dma_start(rows_c[:, :], c.rearrange("(k p) -> k p", p=P)).then_inc(c_in, 16)
            for t in range(NT):
                sp_.dma_start(x_in[:, t, :], x[t * P:(t + 1) * P, :]).then_inc(x_loaded[t], 16)
            ada0_v = w_ada.rearrange("(k p) (m n) -> p k m n", p=P, n=D)
            for q in range(4):
                for j in range(4):
                    for k in (2 * j, 2 * j + 1):
                        sp_.dma_start(ada0[:, q, k, :].rearrange("p (m n) -> p m n", m=2),
                                      ada0_v[:, k, 0:2, 256 * q:256 * q + 256]).then_inc(ada0_in[q][j], 16)
                if q == 0:
                    sp_.dma_start(rows_b[0:16, :], conv_w.rearrange("w (t p) -> (w t) p", p=P))\
                        .then_inc(consts_in, 16)
                    for i, v in enumerate((conv_b, lru_b_x, lru_b_a, lru_lambda)):
                        sp_.dma_start(rows_b[16 + 4 * i:20 + 4 * i, :], v.rearrange("(t p) -> t p", p=P))\
                            .then_inc(consts_in, 16)
                    sp_.dma_start(rows_a[0:72, :], b_ada.rearrange("(t p) -> t p", p=P)).then_inc(consts_in, 16)
                    sp_.dma_start(rows_a[72:120, :], norm_gain.rearrange("s (t p) -> (s t) p", p=P))\
                        .then_inc(consts_in, 16)
                if q < 2:
                    load_n(2 * q)
                    load_n(2 * q + 1)
            for n in range(4, 8):
                load_n(n)
            sp_.wait_ge(wbd_zero, 1)
            for w, dst in ((lru_w_x, wx), (lru_w_a, wa)):
                v = w.rearrange("(t b) i j -> b i t j", b=2)
                for b in range(2):
                    sp_.dma_start(dst[64 * b:64 * b + 64, :, 64 * b:64 * b + 64], v[b])\
                        .then_inc(wbd_in, 16)
            load_group(0, 2)
            for k in range(KD):
                load_ada(4, k, k)
            with sp_.Fori(0, 9) as i:
                for b in range(2):
                    load_group(0, 2 * i + (3 + b))
                    for k in range(4 * b, 4 * b + 4):
                        load_ada(5 + i, k, 8 * i + (8 + k))
            load_group(0, KF - 1)
            for k in range(KD):
                load_ada(14, k, 80 + k)
            for j in range(PHASES[1][1] * PHASES[1][2]):
                g, cc = divmod(j, KF // 2)
                if g < 3 and cc in (2, 6):
                    for k in range(cc - 2, cc + 2):
                        load_ada(15 + g, k, 8 * (11 + g) + k)
                load_n(START[1] + j)
            for n in range(START[2], START[4] + 12):
                load_n(n)
            with sp_.Fori(0, 9) as i:
                for b in range(2):
                    load_group(4, 2 * i + (3 + b))
            load_group(4, KF - 1)
            for n in range(START[5], START[6]):
                load_n(n)
            for half in range(2):
                for t in range(NT):
                    if t % 2 == 0:
                        sp_.wait_ge(out_a, 2 * half + t // 2 + 1)
                    else:
                        sp_.wait_ge(out_v, 2 * half + t // 2 + 1)
                    sp_.dma_start(out[t * P:(t + 1) * P, half * 512:half * 512 + 512],
                                  o_st[:, t, half * 512:half * 512 + 512]).then_inc(out_done, 16)
            sp_.wait_ge(out_done, 16 * 2 * NT)

        @block.gpsimd
        def _(pool):
            nc.gpsimd.memset(ident[:], 0.0).then_inc(pool_consts, 1)
            pool.wait_ge(pool_consts, 1)
            nc.gpsimd.affine_select(out=ident[:], in_=ident[:], compare_op=ALU.not_equal, fill=1.0,
                                    base=0, pattern=[[-1, P]], channel_multiplier=1)\
                .then_inc(pool_consts, 1)
            nc.gpsimd.memset(ones[:], 1.0).then_inc(pool_consts, 1)
            nc.gpsimd.memset(eps[:], EPS).then_inc(pool_consts, 1)
            nc.gpsimd.iota(iot[:, 0, :], [[-1, S]], base=S - P, channel_multiplier=1)\
                .then_inc(pool_iota, 1)
            nc.gpsimd.memset(wx[:], 0.0)
            nc.gpsimd.memset(wa[:], 0.0).then_inc(wbd_zero, 1)

        @block.tensor
        def _(pe):
            def products(slot, kk, bank0, moving, start, stop):
                hi, lo = moving
                for b in range(2):
                    o = ps[bank0 + b][:, :]
                    col = kk * 256 + b * P
                    wh, wl = w_hi[:, slot, col:col + P], w_lo[:, slot, col:col + P]
                    nc.tensor.matmul(o, wh, hi, start=start, stop=False)
                    nc.tensor.matmul(o, wh, lo, start=False, stop=False)
                    last = nc.tensor.matmul(o, wl, hi, start=False, stop=stop)
                return last

            def over_h(n, slot, c, parity, h_tiles=None):
                pe.wait_ge(lo_done, n + 1)
                for kk in range(2):
                    k = 2 * c + kk
                    if h_tiles is not None:
                        pe.wait_ge(h_ready, h_tiles + k + 1)
                    last = products(slot, kk, 2 * parity, (h_hi[:, k, :], h_lo[:, k, :]), k == 0,
                                    k == KD - 1)
                last.then_inc(chunk_used, 1)

            def sum_mod(col, pieces):
                pe.wait_ge(ada_done, pieces)
                for j in range(4):
                    dst = bank_mod[:, bass.ds(4 * col + j, 1)]
                    last = nc.tensor.matmul(dst, ada_acc[:, 0, j * P:(j + 1) * P], ones[:, 0:1],
                                            start=True, stop=True)
                last.then_inc(ada_col, 1)

            def sum_squares(s):
                for k in range(KD):
                    pe.wait_ge(sq_ready, 8 * (s - 1) + k + 1)
                    if k == 0:
                        pe.wait_ge(rms_ready, 2 * s)
                    for t in range(NT):
                        last = nc.tensor.matmul(bank_stat[:, t:t + 1], tmp[:, k % 3, t * P:(t + 1) * P],
                                                ones[:, 0:1], start=(k == 0 and t == 0),
                                                stop=(k == KD - 1), skip_group_check=True)
                    last.then_inc(ss_done, 1)

            def sum_y(s):
                pe.wait_ge(yacc_done, 8 * (s + 1))
                for t in range(NT):
                    last = nc.tensor.matmul(bank_stat[:, t:t + 1], yacc[:, t * P:(t + 1) * P], ones[:, 0:1],
                                            start=True, stop=True)
                last.then_inc(ysum_done, 1)

            def spread(j):
                pe.wait_ge(diag_ready, j + 1)
                nc.tensor.matmul(bank_r[:, :], ones[:, :], diag[:, :, :], start=True, stop=True)\
                    .then_inc(rstd_ready, 1)

            def sum_mod0(q):
                bank = (bank_mod, bank_tr)[q % 2]
                if q == 0:
                    pe.wait_ge(silu_c_ready, 1)
                elif q == 1:
                    pe.wait_ge(cols_ready, 1)
                else:
                    pe.wait_ge(mod0_ready, q - 1)
                for k in range(KD - ADA_PE, KD):
                    if k % 2 == 0 or k == KD - ADA_PE:
                        pe.wait_ge(ada0_in[q][k // 2], 32)
                    for j in range(4):
                        nc.tensor.matmul(bank[:, j:j + 1], ada0[:, q, k, j * P:(j + 1) * P],
                                         silu_c[:, 2, k:k + 1], start=(k == KD - ADA_PE and j == 0),
                                         stop=False, skip_group_check=True)
                pe.wait_ge(ada0_done, q + 1)
                for j in range(4):
                    last = nc.tensor.matmul(bank[:, j:j + 1], ada_acc[:, q % 2, j * P:(j + 1) * P],
                                            ones[:, 0:1], start=False, stop=True, skip_group_check=True)
                last.then_inc(mod0_sum, 1)

            def ffn(f):
                ph = 4 * f
                n0 = START[ph]

                def group(g, parity):
                    pe.wait_ge(hid_f_done, g + (KF * f - 1))
                    for c in range(4):
                        over_h(4 * g + (n0 + c), c, c, parity)

                group(2, 0)
                if f == 0:
                    sum_mod(4, 8)
                with pe.Fori(0, 9) as i:
                    for b in range(2):
                        group(2 * i + (3 + b), 1 - b)
                    if f == 0:
                        sum_mod(5 + i, 8 * i + 16)
                group(KF - 1, 1)
                if f == 0:
                    sum_mod(14, 88)
                ph += 1
                n0 = START[ph]
                for g in range(4):
                    if g < 2:
                        pe.wait_ge(hid_f_done, KF * (f + 1) - 1 + g)
                    else:
                        pe.wait_ge(y_done, 16 * f + 2 * (g - 1))

                    def over_hid(n, c, slot, start=False, stop=False):
                        pe.wait_ge(lo_done, n + 1)
                        for kk in range(2):
                            k = 2 * c + kk
                            if g == 0:
                                pe.wait_ge(hid_ready, k + (KF * f + 1))
                            if isinstance(k, int):
                                moving = hid_hi[:, k, :], hid_lo[:, k, :]
                            else:
                                moving = hid_hi[:, bass.ds(k, 1), :], hid_lo[:, bass.ds(k, 1), :]
                            last = products(slot, kk, 2 * (g % 2), moving, start and kk == 0,
                                            stop and kk == 1)
                        last.then_inc(chunk_used, 1)

                    n = n0 + 11 * g
                    over_hid(n, 0, 0, start=True)
                    with pe.Fori(0, 2) as i:
                        for j in range(1, 5):
                            over_hid(4 * i + (n + j), 4 * i + j, j % SLOTS)
                    over_hid(n + 9, 9, 1)
                    over_hid(n + 10, 10, 2, stop=True)
                    if f == 0 and g < 3:
                        sum_mod(15 + g, 96 + 8 * g)

            pe.wait_ge(pool_consts, 4)
            pe.wait_ge(c_in, 16)
            nc.tensor.transpose(bank_tr[:, 168:176], rows_c[:, :], ident[0:KD, 0:KD]).then_inc(c_tr, 1)
            for t in range(NT):
                pe.wait_ge(x_loaded[t], 16)
            for k in range(KD):
                if k >= 4:
                    pe.wait_ge(x0_ready, k - 3)
                for t in range(NT):
                    last = nc.tensor.transpose(ps[k % 4][:, t * P:(t + 1) * P],
                                               x_in[:, t, k * P:(k + 1) * P], ident[:, :])
                last.then_inc(x_tr, 1)
            pe.wait_ge(consts_in, 16 * 7)
            pe.wait_ge(c_ready, 1)
            nc.tensor.transpose(bank_tr[:, 0:120], rows_a[:, :], ident[0:120, 0:120])
            nc.tensor.transpose(bank_tr[:, 128:160], rows_b[:, :], ident[0:32, 0:32]).then_inc(cols_tr, 1)
            spread(0)
            sum_mod0(0)
            for q in range(4):
                if q < 3:
                    sum_mod0(q + 1)
                if q == 0:
                    pe.wait_ge(x0_ready, KD)
                for g in range(2):
                    over_h(2 * q + g, (2 * q + g) % SLOTS, q, g, 0)
            ffn(0)
            sum_y(0)
            spread(1)
            sum_squares(1)
            spread(2)

            def vtr(t):
                pe.wait_ge(mix_evac, AT[4 + t // 2] + 1)
                if t == 2:
                    pe.wait_ge(lru_a_done, 4)
                elif t:
                    pe.wait_ge(v_ready, t)
                for j in range(NT):
                    last = nc.tensor.transpose(bank_g[:, j * P:(j + 1) * P], vT[:, t % 2, j * P:(j + 1) * P],
                                               ident[:, :])
                last.then_inc(v_tr, 1)

            def att_step(i):
                if i < NU:
                    h, qt = divmod(i, NT)
                    p, r = h // 2, HD * (h % 2)
                    if i:
                        pe.wait_ge(negs_done, i)
                    if h % 4 == 0 and qt == 0:
                        pe.wait_ge(mix_evac, AT[2 + h // 4] + 1)
                    nc.tensor.matmul(bank_s[:, 0:(qt + 1) * P], qT[r:r + HD, p, qt * P:(qt + 1) * P],
                                     kT[r:r + HD, p, 0:(qt + 1) * P], start=True, stop=True)\
                        .then_inc(s_done, 1)
                if 0 <= i - T_LAG < NU:
                    u = i - T_LAG
                    qt = u % NT
                    pe.wait_ge(p_ready, u + 1)
                    if u:
                        pe.wait_ge(pt_ready, u)
                    for j in range(qt + 1):
                        last = nc.tensor.transpose(bank_pt[:, j * P:(j + 1) * P],
                                                   att[:, u % 4, j * P:(j + 1) * P], ident[:, :])
                    last.then_inc(pt_done, 1)
                if i >= PV_LAG:
                    u = i - PV_LAG
                    h, qt = divmod(u, NT)
                    p, r = h // 2, HD * (h % 2)
                    pe.wait_ge(pt_ready, u + 1)
                    if u % 16 == 0:
                        pe.wait_ge(v_ready, 2 if u == 0 else 4)
                    if u and u % 8 == 0:
                        pe.wait_ge(o_lo_done, p)
                    for j in range(qt + 1):
                        last = nc.tensor.matmul(bank_o[r:r + HD, qt * P:(qt + 1) * P],
                                                v_nat[:, j, h * HD:(h + 1) * HD],
                                                pT[:, u % 4, j * P:(j + 1) * P],
                                                start=(j == 0), stop=(j == qt))
                    last.then_inc(pv_done, 1)

            def gate(t, w, n):
                pe.wait_ge(conv_done, t + 1)
                if n == 0:
                    pe.wait_ge(wbd_in, 64)
                    pe.wait_ge(v_ready, 2)
                elif n % 2:
                    pe.wait_ge(tx_done, n // 2 + 1)
                else:
                    pe.wait_ge(lru_a_done, n // 2)
                nc.tensor.matmul(bank_g[:, :], w[:, t, :], xc[t % 2], start=True, stop=True)\
                    .then_inc(gate_done, 1)

            for hp in range(112):
                n = START[2] + hp // 2
                ph, g, c, slot, _ = locate(n)
                kk = hp % 2
                k = 2 * c + kk
                if kk == 0:
                    pe.wait_ge(lo_done, n + 1)
                if ph == 2:
                    if hp < 16:
                        pe.wait_ge(h_ready, 8 + k + 1)
                    elif k == 0 and g < 10:
                        pe.wait_ge(mix_evac if MIX_ORDER[g - 2] < 8 else gel_done,
                                   g - 1 if MIX_ORDER[g - 2] < 8 else 2)
                    moving = h_hi[:, k, :], h_lo[:, k, :]
                    start, stop = k == 0, k == KD - 1
                else:
                    if g < 2 and hp % 8 == 0:
                        pe.wait_ge(gel_done, 2 if g == 0 else 4)
                    if g >= 2 and hp % 8 == 0:
                        pe.wait_ge(y_done, 8 + 2 * (g - 1))
                    if g == 0:
                        if k < 4:
                            pe.wait_ge(o_lo_done, k + 1)
                        else:
                            pe.wait_ge(rec_ready, k - 3)
                    moving = mix_hi[:, k, :], mix_lo[:, k, :]
                    start, stop = hp % 8 == 0, hp % 8 == 7
                last = products(slot, kk, 2 * (g % 2), moving, start, stop)
                if kk == 1:
                    last.then_inc(chunk_used, 1)
                for e, arg in EVENTS.get(hp, ()):
                    if e == "vtr":
                        vtr(arg)
                    elif e == "att":
                        att_step(arg)
                    elif e == "gate_x":
                        gate(arg, wx, 2 * arg)
                    elif e == "gate_a":
                        gate(arg, wa, 2 * arg + 1)
            sum_y(1)
            spread(3)
            sum_squares(2)
            spread(4)
            for n in range(START[4], START[4] + 8):
                ph, g, c, slot, _ = locate(n)
                over_h(n, slot, c, g, 16)
            ffn(1)
            sum_y(2)
            spread(5)
            for k in range(KD):
                pe.wait_ge(xt_ready, 16 + k + 1)
                if k == 0:
                    pe.wait_ge(y_done, 24)
                if k == 4:
                    pe.wait_ge(t_ready, 24)
                for t in range(NT):
                    last = nc.tensor.transpose(ps[t + 4 * (k // 4)][:, (k % 4) * P:(k % 4 + 1) * P],
                                               xT[:, k, t * P:(t + 1) * P], ident[:, :])
                last.then_inc(out_tr, 1)

        @block.scalar
        def _(act):
            def cut(s, n, b, loaded):
                act.wait_ge(raw_in[s], loaded)
                if not isinstance(n, int) or n - b >= 0:
                    act.wait_ge(chunk_used, n - b + 1)
                nc.scalar.activation(w_hi[:, s, :], raw[:, s, :], ACT.Copy).then_inc(hi_done, 1)

            def cut_hi_n(n):
                ph, _, _, s, b = locate(n)
                g, j = divmod(n - START[ph], PHASES[ph][2])
                cut(s, n, b, filled(ph, g, j))

            def cut_hi_group(ph, g, chunks=range(4)):
                for c in chunks:
                    cut(c, number(ph, g, c), 4, filled(ph, g, c))

            def squares(s):
                for k in range(KD):
                    act.wait_ge(xt_ready, 8 * (s - 1) + k + 1)
                    if k >= 3:
                        act.wait_ge(ss_done, 8 * (s - 1) + k - 2)
                    nc.scalar.activation(tmp[:, k % 3, :], xT[:, k, :], ACT.Square).then_inc(sq_ready, 1)

            def root(j, wait_sem, value):
                act.wait_ge(wait_sem, value)
                nc.scalar.activation(rms[:, j % 2, :], bank_stat[:, 0:NT], ACT.Sqrt, bias=eps[:, 0:1],
                                     scale=1.0 / D).then_inc(rms_ready, 1)

            def cut_h(s, k):
                act.wait_ge(h_scaled, 8 * s + k + 1)
                m = 24 * s + k
                nc.scalar.activation(h_hi[:, k, :], tmp[:, k % 3, :], ACT.Identity,
                                     bias=mod[:, m:m + 1]).then_inc(h_hi_done, 1)

            def cut_all_h(s, n0):
                for k in range(KD):
                    if k >= 4:
                        cut_hi_n(n0 + k)
                    cut_h(s, k)

            def swiglu(f, g, parity, first):
                ahead = 7 if isinstance(g, int) and g == 0 else 4
                act.wait_ge(chunk_used, 4 * g + (START[4 * f] + ahead))
                if not first:
                    act.wait_ge(hid_f_done, KF * f + g)
                nc.scalar.activation(tmp[:, 0, :], ps[2 * parity][:, :], ACT.Tanh, scale=0.5)\
                    .then_inc(tanh_done, 1)
                act.wait_ge(hid_f_done, KF * f + g + 1)
                dst = hid_hi[:, g, :] if isinstance(g, int) else hid_hi[:, bass.ds(g, 1), :]
                src = hid_f[:, :] if isinstance(g, int) else hid_f[:, :].rearrange("p (o s) -> p o s", o=1)
                nc.scalar.activation(dst, src, ACT.Copy).then_inc(hid_hi_done, 1)

            def take_y(s, ph, g):
                act.wait_ge(chunk_used, number(ph, g, PHASES[ph][2] - 1) + 1)
                for b in range(2):
                    m = 2 * g + b
                    if m >= 2:
                        act.wait_ge(yacc_done, 8 * s + m - 1)
                    nc.scalar.activation(tmp[:, b, :], ps[2 * (g % 2) + b][:, :], ACT.Square)\
                        .then_inc(ysq_done, 1)
                for b in range(2):
                    nc.scalar.activation(y[:, 2 * g + b, :], ps[2 * (g % 2) + b][:, :], ACT.Copy)\
                        .then_inc(y_done, 1)

            def ffn(f):
                ph = 4 * f
                cut_hi_group(ph, 2, range(3))
                swiglu(f, 0, 0, f == 0)
                cut_hi_group(ph, 2, range(3, 4))
                swiglu(f, 1, 1, False)
                with act.Fori(0, 9) as i:
                    for b in range(2):
                        cut_hi_group(ph, 2 * i + (3 + b))
                        swiglu(f, 2 * i + (2 + b), b, False)
                cut_hi_group(ph, KF - 1)
                swiglu(f, KF - 2, 0, False)
                ph += 1
                for j in range(PHASES[ph][1] * PHASES[ph][2]):
                    g, c = divmod(j, KF // 2)
                    cut_hi_n(START[ph] + j)
                    if c == 3:
                        if g == 0:
                            swiglu(f, KF - 1, 1, False)
                        else:
                            take_y(2 * f, ph, g - 1)
                if f == 0:
                    cut_hi_n(START[2])
                    cut_hi_n(START[2] + 1)
                take_y(2 * f, ph, 3)

            act.wait_ge(c_ready, 1)
            nc.scalar.activation(silu_c[:, 0, :], silu_c[:, 1, :], ACT.Tanh, scale=0.5).then_inc(tanh_c, 1)
            for t in range(NT):
                act.wait_ge(x_loaded[t], 16)
                nc.scalar.activation(h_lo[:, 2 * t:2 * t + 2, :].rearrange("p k s -> p (k s)"),
                                     x_in[:, t, :], ACT.Square, accum_out=x_ss[:, t:t + 1])\
                    .then_inc(x_summed, 1)
            act.wait_ge(x_summed, NT)
            nc.scalar.activation(rms[:, 0, :], x_ss[:, :], ACT.Sqrt, bias=eps[:, 0:1], scale=1.0 / D)\
                .then_inc(rms_ready, 1)
            for k in range(KD):
                act.wait_ge(x_tr, k + 1)
                nc.scalar.activation(xT[:, k, :], ps[k % 4][:, :], ACT.Copy).then_inc(x0_ready, 1)
            act.wait_ge(lam_abs, 1)
            nc.scalar.activation(sp[:, 1, :], sp[:, 0, :], ACT.Exp, scale=-1.0).then_inc(tanh_c, 1)
            for q in range(4):
                cut_hi_n(2 * q)
                cut_hi_n(2 * q + 1)
                act.wait_ge(mod0_ready, q + 1)
                cut_h(0, 2 * q)
                cut_h(0, 2 * q + 1)
            ffn(0)

            root(1, ysum_done, 1)
            cut_hi_n(START[2] + 2)
            cut_hi_n(START[2] + 3)
            squares(1)
            root(2, ss_done, 8)
            cut_all_h(1, START[2])

            def evac(gi):
                grp = MIX_ORDER[gi]
                act.wait_ge(chunk_used, START[2] + (7 if gi == 0 else 4 * gi + 4))
                if grp == 6:
                    act.wait_ge(xr_zero, 1)
                if grp == 5:
                    act.wait_ge(v_tr, 2)
                for b in range(2):
                    t = 2 * (grp % 2) + b if grp // 2 != 2 else b
                    src = ps[2 * (gi % 2) + b][:, :]
                    if grp < 6:
                        dst = (qT, kT, vT)[grp // 2][:, t, :]
                    else:
                        dst = xr[:, t, 3:3 + S]
                    last = nc.scalar.activation(dst, src, ACT.Copy)
                last.then_inc(mix_evac, 1)

            def vtr(t):
                act.wait_ge(v_tr, t + 1)
                nc.scalar.activation(v_nat[:, :, t * P:(t + 1) * P],
                                     bank_g[:, :].rearrange("p (j f) -> p j f", j=NT), ACT.Copy)\
                    .then_inc(v_ready, 1)

            def att_step(i):
                if i < NU:
                    w = (i % NT + 1) * P
                    act.wait_ge(negs_done, i + 1)
                    nc.scalar.activation(att[:, i % 4, 0:w], att[:, i % 4, 0:w], ACT.Exp,
                                         bias=neg_max[:, i % 4, :], scale=-1.0,
                                         accum_out=den[:, i % 4, :]).then_inc(exp_done, 1)
                if 0 <= i - T_LAG < NU:
                    u = i - T_LAG
                    w = (u % NT + 1) * P
                    act.wait_ge(pt_done, u + 1)
                    if u >= 4:
                        act.wait_ge(pv_done, u - 3)
                    nc.scalar.activation(pT[:, u % 4, 0:w], bank_pt[:, 0:w], ACT.Copy).then_inc(pt_ready, 1)
                if i % 8 == (7 + PV_LAG) % 8 and i >= 7 + PV_LAG:
                    p = (i - 7 - PV_LAG) // 8
                    act.wait_ge(pv_done, 8 * p + 8)
                    nc.scalar.activation(mix_hi[:, p, :], bank_o[:, :], ACT.Copy).then_inc(o_hi_done, 1)

            def gate_x(t):
                act.wait_ge(gate_done, 2 * t + 1)
                if t >= 2:
                    act.wait_ge(scan_done, t - 1)
                nc.scalar.activation(tx[t % 2], bank_g[:, :], ACT.Tanh, bias=half_b[:, 0, t:t + 1],
                                     scale=0.5).then_inc(tx_done, 1)

            def gate_a(t):
                act.wait_ge(gate_done, 2 * t + 2)
                if t:
                    act.wait_ge(om_done, t)
                else:
                    act.wait_ge(h_ready, 16)
                nc.scalar.activation(tmp[:, 0, :], bank_g[:, :], ACT.Tanh, bias=half_b[:, 1, t:t + 1],
                                     scale=0.5).then_inc(act_step, 1)
                act.wait_ge(act_step, t + 1)
                nc.scalar.activation(tmp[:, 1, :], tmp[:, 0, :], ACT.Tanh, bias=sp[:, 6, t:t + 1],
                                     scale=sp[:, 6, t:t + 1])
                nc.scalar.activation(aa[t % 2], tmp[:, 0, :], ACT.Exp, bias=sp[:, 7, t:t + 1],
                                     scale=sp[:, 7, t:t + 1]).then_inc(lru_a_done, 1)

            def scan(pair):
                act.wait_ge(om_done, 2 * pair + 2)
                for b in range(2):
                    nc.scalar.activation(om[b], om[b], ACT.Sqrt).then_inc(sqrt_done, 1)

            def gelu(t):
                act.wait_ge(chunk_used, START[2] + 4 * AT[8 + t // 2] + 4)
                bank = ps[2 * (AT[8 + t // 2] % 2) + t % 2]
                if t == 0:
                    act.wait_ge(om_done, 4)
                else:
                    act.wait_ge(gel_done, t)
                nc.scalar.activation(tmp[:, 0, :], bank[:, :], ACT.Square).then_inc(gsq_done, 1)
                act.wait_ge(gu_done, t + 1)
                nc.scalar.activation(tmp[:, 0, :], tmp[:, 0, :], ACT.Tanh,
                                     scale=float(np.sqrt(2 / np.pi))).then_inc(gt_done, 1)

            def rec(t):
                act.wait_ge(rec_f_done, t + 1)
                nc.scalar.activation(mix_hi[:, 4 + t, :], tmp[:, 1, :], ACT.Copy).then_inc(rec_hi_done, 1)

            def run_events(hp):
                for e, arg in EVENTS.get(hp, ()):
                    if e == "evac":
                        evac(arg)
                    elif e == "vtr":
                        vtr(arg)
                    elif e == "att":
                        att_step(arg)
                    elif e == "gate_x":
                        gate_x(arg)
                    elif e == "gate_a":
                        gate_a(arg)
                    elif e == "scan":
                        scan(arg)
                    elif e == "gelu":
                        gelu(arg)
                    elif e == "rec":
                        rec(arg)

            for hp in range(112):
                n = START[2] + hp // 2
                if hp >= 10 and hp % 2 == 0 and n < START[4] - 1:
                    cut_hi_n(n + 3)
                if hp >= 88 and hp % 8 == 0:
                    take_y(1, 3, (hp - 80) // 8 - 1)
                run_events(hp)
            take_y(1, 3, 3)
            root(3, ysum_done, 2)
            cut_hi_n(START[4] + 2)
            cut_hi_n(START[4] + 3)
            squares(2)
            root(4, ss_done, 16)
            cut_all_h(2, START[4])
            ffn(1)
            root(5, ysum_done, 3)
            for half in range(2):
                for t in (0, 2):
                    act.wait_ge(out_tr, 4 * half + 4)
                    nc.scalar.activation(o_st[:, t, half * 512:half * 512 + 512], ps[t + 4 * half][:, :],
                                         ACT.Copy).then_inc(out_a, 1)

        @block.vector
        def _(dve):
            steps = [0]

            def link(ins):
                steps[0] += 1
                ins.then_inc(dve_step, 1)
                dve.wait_ge(dve_step, steps[0])

            def cut(s, n):
                dve.wait_ge(hi_done, n + 1)
                nc.vector.tensor_tensor(w_lo[:, s, :], raw[:, s, :], w_hi[:, s, :].bitcast(F32),
                                        ALU.subtract).then_inc(lo_done, 1)

            def cut_lo_n(n):
                cut(locate(n)[3], n)

            def cut_lo_group(ph, g, chunks=range(4)):
                for c in chunks:
                    cut(c, number(ph, g, c))

            def ada(col, k, a):
                s = k % SLOTS
                dve.wait_ge(ada_in[s], 32 * (col - 4) + 16 * (k // SLOTS + 1))
                acc = ada_acc[:, 0, :]
                if k == 0:
                    if not isinstance(col, int) or col > 4:
                        dve.wait_ge(ada_col, col - 4)
                    nc.vector.tensor_scalar(acc, ada_raw[:, s, :], silu_c[:, 2, 0:1], None, ALU.mult)\
                        .then_inc(ada_done, 1)
                else:
                    dve.wait_ge(ada_done, a)
                    nc.vector.scalar_tensor_tensor(acc, ada_raw[:, s, :], silu_c[:, 2, k:k + 1], acc,
                                                   ALU.mult, ALU.add).then_inc(ada_done, 1)

            def finish_mod(lo, hi, count):
                dve.wait_ge(ada_col, count)
                link(nc.vector.tensor_tensor(mod[:, lo:hi], bank_mod[:, lo:hi], cols_a[:, lo:hi], ALU.add))

            def make_a(s):
                return nc.vector.scalar_tensor_tensor(A[:, s, :], mod[:, 24 * s + 8:24 * s + 16], 1.0,
                                                      cols_a[:, 72 + 16 * s:80 + 16 * s], ALU.add, ALU.mult)

            def make_g(s):
                link(nc.vector.scalar_tensor_tensor(G[:, s, :], mod[:, 24 * s + 16:24 * s + 24], 1.0,
                                                    cols_a[:, 80 + 16 * s:88 + 16 * s], ALU.add, ALU.mult))
                if s != 1:
                    link(nc.vector.tensor_scalar(G[:, s, :], G[:, s, :], 0.5, None, ALU.mult))

            def inverse_rms(j):
                dve.wait_ge(rms_ready, j + 1)
                link(nc.vector.reciprocal(rms[:, j % 2, :], rms[:, j % 2, :]))
                for t in range(NT):
                    last = nc.vector.tensor_scalar(diag[:, t, :], ident[:, :], rms[:, j % 2, t:t + 1], None,
                                                   ALU.mult)
                last.then_inc(diag_ready, 1)

            def scale_h(s, k):
                if k >= 3:
                    dve.wait_ge(h_ready, 8 * s + k - 2)
                nc.vector.scalar_tensor_tensor(tmp[:, k % 3, :], xT[:, k, :], A[:, s, k:k + 1],
                                               bank_r[:, :], ALU.mult, ALU.mult).then_inc(h_scaled, 1)

            def rest_h(s, k):
                dve.wait_ge(h_hi_done, 8 * s + k + 1)
                m = 24 * s + k
                nc.vector.scalar_tensor_tensor(h_lo[:, k, :], tmp[:, k % 3, :], mod[:, m:m + 1],
                                               h_hi[:, k, :].bitcast(F32), ALU.add,
                                               ALU.subtract).then_inc(h_ready, 1)

            def cut_all_h(s, n0):
                dve.wait_ge(rstd_ready, 2 * s + 1)
                scale_h(s, 0)
                for k in range(KD):
                    if k < KD - 1:
                        scale_h(s, k + 1)
                    if k >= 4:
                        cut_lo_n(n0 + k)
                    rest_h(s, k)

            def residual(s):
                dve.wait_ge(rstd_ready, 2 * s + 2)
                for k in range(KD + 1):
                    if k < KD:
                        nc.vector.scalar_tensor_tensor(y[:, k, :], y[:, k, :], G[:, s, k:k + 1],
                                                       bank_r[:, :], ALU.mult, ALU.mult)\
                            .then_inc(t_ready, 1)
                    if k:
                        dve.wait_ge(t_ready, 8 * s + k)
                        nc.vector.tensor_tensor(xT[:, k - 1, :], xT[:, k - 1, :], y[:, k - 1, :], ALU.add)\
                            .then_inc(xt_ready, 1)

            def silu_up(f, g, parity):
                dve.wait_ge(tanh_done, KF * f + g + 1)
                nc.vector.scalar_tensor_tensor(tmp[:, 1, :], tmp[:, 0, :], 1.0, ps[2 * parity][:, :],
                                               ALU.add, ALU.mult).then_inc(silu_done, 1)
                dve.wait_ge(silu_done, KF * f + g + 1)
                if not isinstance(g, int) or g:
                    dve.wait_ge(hid_ready, KF * f + g)
                nc.vector.scalar_tensor_tensor(hid_f[:, :], tmp[:, 1, :], 0.5, ps[2 * parity + 1][:, :],
                                               ALU.mult, ALU.mult).then_inc(hid_f_done, 1)

            def cut_hid(f, g):
                dve.wait_ge(hid_hi_done, KF * f + g + 1)
                if isinstance(g, int):
                    o, i0, i1 = hid_lo[:, g, :], hid_f[:, :], hid_hi[:, g, :].bitcast(F32)
                else:
                    o, i1 = hid_lo[:, bass.ds(g, 1), :], hid_hi[:, bass.ds(g, 1), :].bitcast(F32)
                    i0 = hid_f[:, :].rearrange("p (o s) -> p o s", o=1)
                nc.vector.tensor_tensor(o, i0, i1, ALU.subtract).then_inc(hid_ready, 1)

            def zero_yacc(hid_tiles):
                dve.wait_ge(hid_ready, hid_tiles)
                nc.vector.memset(yacc[:, :], 0.0).then_inc(yacc_zero, 1)

            def add_y(s, g):
                for b in range(2):
                    m = 2 * g + b
                    dve.wait_ge(ysq_done, 8 * s + m + 1)
                    if m == 0:
                        dve.wait_ge(yacc_zero, s + 1)
                    else:
                        dve.wait_ge(yacc_done, 8 * s + m)
                    nc.vector.tensor_tensor(yacc[:, :], yacc[:, :], tmp[:, b, :], ALU.add)\
                        .then_inc(yacc_done, 1)

            def ffn(f):
                ph = 4 * f
                cut_lo_group(ph, 2, range(3))
                silu_up(f, 0, 0)
                cut_hid(f, 0)
                cut_lo_group(ph, 2, range(3, 4))
                silu_up(f, 1, 1)
                cut_hid(f, 1)
                if f == 0:
                    for k in range(KD):
                        ada(4, k, k)
                with dve.Fori(0, 9) as i:
                    for b in range(2):
                        g = 2 * i + (2 + b)
                        cut_lo_group(ph, g + 1)
                        if f == 0:
                            for k in (4 * b, 4 * b + 1):
                                ada(5 + i, k, 8 * i + (8 + k))
                        silu_up(f, g, b)
                        if f == 0:
                            for k in (4 * b + 2, 4 * b + 3):
                                ada(5 + i, k, 8 * i + (8 + k))
                        cut_hid(f, g)
                cut_lo_group(ph, KF - 1)
                silu_up(f, KF - 2, 0)
                cut_hid(f, KF - 2)
                if f == 0:
                    for k in range(KD):
                        ada(14, k, 80 + k)
                ph += 1
                for j in range(PHASES[ph][1] * PHASES[ph][2]):
                    g, c = divmod(j, KF // 2)
                    cut_lo_n(START[ph] + j)
                    if c == 3:
                        if g == 0:
                            silu_up(f, KF - 1, 1)
                            cut_hid(f, KF - 1)
                            zero_yacc(KF * (f + 1))
                            if f == 0:
                                finish_mod(16, 48, 11)
                                make_g(0)
                                make_g(1)
                                link(make_a(1))
                        else:
                            add_y(2 * f, g - 1)
                    if f == 0 and g < 3 and 4 <= c < 8:
                        for k in (2 * c - 8, 2 * c - 7):
                            ada(15 + g, k, 8 * (11 + g) + k)
                if f == 0:
                    cut_lo_n(START[2])
                    cut_lo_n(START[2] + 1)
                add_y(2 * f, 3)

            dve.wait_ge(c_tr, 1)
            nc.vector.tensor_copy(silu_c[:, 1, :], bank_tr[:, 168:176]).then_inc(c_ready, 1)
            dve.wait_ge(tanh_c, 1)
            link(nc.vector.scalar_tensor_tensor(silu_c[:, 0, :], silu_c[:, 0, :], 1.0, silu_c[:, 1, :],
                                                ALU.add, ALU.mult))
            nc.vector.tensor_scalar(silu_c[:, 2, :], silu_c[:, 0, :], 0.5, None, ALU.mult)\
                .then_inc(silu_c_ready, 1)
            dve.wait_ge(silu_c_ready, 1)

            def softplus():
                dve.wait_ge(tanh_c, 2)
                link(nc.vector.tensor_scalar(sp[:, 3, :], sp[:, 1, :], 2.0, None, ALU.add))
                link(nc.vector.reciprocal(sp[:, 3, :], sp[:, 3, :]))
                link(nc.vector.tensor_tensor(sp[:, 3, :], sp[:, 3, :], sp[:, 1, :], ALU.mult))
                link(nc.vector.tensor_tensor(sp[:, 4, :], sp[:, 3, :], sp[:, 3, :], ALU.mult))
                link(nc.vector.memset(sp[:, 5, :], 1.0 / 17))
                for n in (15, 13, 11, 9, 7, 5, 3, 1):
                    link(nc.vector.tensor_tensor(sp[:, 5, :], sp[:, 5, :], sp[:, 4, :], ALU.mult))
                    link(nc.vector.tensor_scalar(sp[:, 5, :], sp[:, 5, :], 1.0 / n, None, ALU.add))
                link(nc.vector.tensor_tensor(sp[:, 5, :], sp[:, 5, :], sp[:, 3, :], ALU.mult))
                link(nc.vector.tensor_scalar(sp[:, 2, :], sp[:, 2, :], 0.0, 0.5, ALU.max, ALU.mult))
                link(nc.vector.tensor_tensor(sp[:, 5, :], sp[:, 5, :], sp[:, 2, :], ALU.add))
                link(nc.vector.tensor_scalar(sp[:, 6, :], sp[:, 5, :], 8.0, None, ALU.mult))
                link(nc.vector.tensor_scalar(sp[:, 7, :], sp[:, 5, :], -8.0, None, ALU.mult))
                link(nc.vector.tensor_scalar(half_b[:, 0, :], cols_b[:, 28:32], 0.5, None, ALU.mult))
                link(nc.vector.tensor_scalar(half_b[:, 1, :], cols_b[:, 32:36], 0.5, None, ALU.mult))

            def make_mask():
                dve.wait_ge(pool_iota, 1)
                for n, bits in ((1, 3), (2, 15)):
                    link(nc.vector.tensor_scalar(iot[:, n, :], iot[:, 0, :], bits, None, ALU.bitwise_and))
                link(nc.vector.tensor_copy(cnt[:, 0, :], iot[:, 0, :]))
                link(nc.vector.tensor_scalar(cnt[:, 1, :], cnt[:, 0, :], 128.0, None, ALU.is_le))
                for n in (1, 2):
                    link(nc.vector.tensor_copy(cnt[:, 2, :], iot[:, n, :]))
                    link(nc.vector.scalar_tensor_tensor(cnt[:, 1, :], cnt[:, 2, :], 0.0, cnt[:, 1, :],
                                                        ALU.is_equal, ALU.add))
                link(nc.vector.scalar_tensor_tensor(cnt[:, 1, :], cnt[:, 0, :], 0.0, cnt[:, 1, :],
                                                    ALU.is_ge, ALU.mult))
                link(nc.vector.tensor_scalar(mask[:, :], cnt[:, 1, :], 0.0, -8e30, ALU.is_equal, ALU.mult))
                for n in (2, 3):
                    link(nc.vector.tensor_scalar(cnt[:, 2, :], cnt[:, 1, :], float(n), float(8 * np.log(n)),
                                                 ALU.is_equal, ALU.mult))
                    link(nc.vector.tensor_tensor(mask[:, :], mask[:, :], cnt[:, 2, :], ALU.add))

            def ada0_quarter(q):
                acc = ada_acc[:, q % 2, :]
                if q >= 2:
                    dve.wait_ge(mod0_sum, q - 1)
                for k in range(KD - ADA_PE):
                    if k % 2 == 0:
                        dve.wait_ge(ada0_in[q][k // 2], 32)
                    if k == 0:
                        last = nc.vector.tensor_scalar(acc, ada0[:, q, k, :], silu_c[:, 2, 0:1], None,
                                                       ALU.mult)
                    else:
                        last = nc.vector.scalar_tensor_tensor(acc, ada0[:, q, k, :], silu_c[:, 2, k:k + 1],
                                                              acc, ALU.mult, ALU.add)
                    if k < KD - ADA_PE - 1:
                        link(last)
                last.then_inc(ada0_done, 1)

            def mod0_quarter(q):
                bank = (bank_mod, bank_tr)[q % 2]
                dve.wait_ge(mod0_sum, q + 1)
                two = lambda v: v.rearrange("p (m k) -> p m k", m=2)[:, :, 2 * q:2 * q + 2]
                link(nc.vector.tensor_tensor(two(mod[:, 0:16]), bank[:, 0:4].rearrange("p (m k) -> p m k", m=2),
                                             two(cols_a[:, 0:16]), ALU.add))
                k = 2 * q
                nc.vector.scalar_tensor_tensor(A[:, 0, k:k + 2], mod[:, 8 + k:10 + k], 1.0,
                                               cols_a[:, 72 + k:74 + k], ALU.add, ALU.mult)\
                    .then_inc(mod0_ready, 1)
                dve.wait_ge(mod0_ready, q + 1)

            make_mask()
            inverse_rms(0)
            ada0_quarter(0)
            dve.wait_ge(cols_tr, 1)
            link(nc.vector.tensor_copy(cols_b[:, 8:40], bank_tr[:, 128:160]))
            nc.vector.tensor_copy(cols_a[:, :], bank_tr[:, 0:120]).then_inc(cols_ready, 1)
            dve.wait_ge(cols_ready, 1)
            lam = cols_b[:, 36:40]
            link(nc.vector.tensor_scalar(sp[:, 2, :], lam, -1.0, None, ALU.mult))
            nc.vector.tensor_tensor(sp[:, 0, :], sp[:, 2, :], lam, ALU.max).then_inc(lam_abs, 1)
            for q in range(4):
                if q < 3:
                    ada0_quarter(q + 1)
                mod0_quarter(q)
                if q == 0:
                    dve.wait_ge(rstd_ready, 1)
                    dve.wait_ge(x0_ready, KD)
                scale_h(0, 2 * q)
                scale_h(0, 2 * q + 1)
                cut_lo_n(2 * q)
                rest_h(0, 2 * q)
                cut_lo_n(2 * q + 1)
                rest_h(0, 2 * q + 1)
            ffn(0)

            inverse_rms(1)
            cut_lo_n(START[2] + 2)
            cut_lo_n(START[2] + 3)
            residual(0)
            inverse_rms(2)
            cut_all_h(1, START[2])
            softplus()
            finish_mod(48, 72, 14)
            link(make_a(2))
            make_g(2)
            for t in range(CT):
                last = nc.vector.memset(xr[:, t, 0:3], 0.0)
            last.then_inc(xr_zero, 1)

            def att_step(i):
                if 1 <= i <= NU:
                    u = i - 1
                    w = (u % NT + 1) * P
                    dve.wait_ge(exp_done, u + 1)
                    link(nc.vector.reciprocal(rden[:, u % 4, :], den[:, u % 4, :]))
                    nc.vector.tensor_scalar(att[:, u % 4, 0:w], att[:, u % 4, 0:w], rden[:, u % 4, :],
                                            None, ALU.mult).then_inc(p_ready, 1)
                if i < NU:
                    qt = i % NT
                    w = (qt + 1) * P
                    dve.wait_ge(s_done, i + 1)
                    if i >= 4:
                        dve.wait_ge(pt_done, i - 3)
                    nc.vector.tensor_tensor_reduce(out=att[:, i % 4, 0:w], in0=bank_s[:, 0:w],
                                                   in1=mask[:, S - w:S], scale=-1.0 / 8, scalar=3e38,
                                                   op0=ALU.add, op1=ALU.min,
                                                   accum_out=neg_max[:, i % 4, :]).then_inc(negs_done, 1)
                if i % 8 == (7 + PV_LAG) % 8 and i >= 7 + PV_LAG:
                    p = (i - 7 - PV_LAG) // 8
                    dve.wait_ge(o_hi_done, p + 1)
                    nc.vector.tensor_tensor(mix_lo[:, p, :], bank_o[:, :], mix_hi[:, p, :].bitcast(F32),
                                            ALU.subtract).then_inc(o_lo_done, 1)

            def conv(t):
                dve.wait_ge(mix_evac, AT[6 + t // 2] + 1)
                if t >= 2:
                    dve.wait_ge(gate_done, 2 * t - 2)
                w = 8 + t
                link(nc.vector.tensor_scalar(xc[t % 2], xr[:, t, 0:S], cols_b[:, w:w + 1],
                                             cols_b[:, 24 + t:25 + t], ALU.mult, ALU.add))
                for tap in range(1, TAPS):
                    w += CT
                    last = nc.vector.scalar_tensor_tensor(xc[t % 2], xr[:, t, tap:tap + S],
                                                          cols_b[:, w:w + 1], xc[t % 2], ALU.mult, ALU.add)
                    if tap < TAPS - 1:
                        link(last)
                last.then_inc(conv_done, 1)

            def gate_a(t):
                dve.wait_ge(lru_a_done, t + 1)
                if t >= 2:
                    pass
                link(nc.vector.tensor_tensor(om[t % 2], aa[t % 2], aa[t % 2], ALU.mult))
                nc.vector.scalar_tensor_tensor(om[t % 2], om[t % 2], 1.0, tmp[:, 1, :], ALU.add,
                                               ALU.mult).then_inc(om_done, 1)

            def scan(pair):
                for b in range(2):
                    t = 2 * pair + b
                    dve.wait_ge(tx_done, t + 1)
                    dve.wait_ge(conv_done, t + 1)
                    link(nc.vector.scalar_tensor_tensor(tx[b], tx[b], 1.0, xc[b], ALU.add, ALU.mult))
                    dve.wait_ge(sqrt_done, t + 1)
                    link(nc.vector.scalar_tensor_tensor(tx[b], tx[b], 0.5, om[b], ALU.mult, ALU.mult))
                    nc.vector.tensor_tensor_scan(xr[:, t, 3:3 + S], aa[b], tx[b], 0.0, ALU.mult,
                                                 ALU.add).then_inc(scan_done, 1)

            def gelu(t):
                bank = ps[2 * (AT[8 + t // 2] % 2) + t % 2]
                dve.wait_ge(gsq_done, t + 1)
                link(nc.vector.tensor_scalar(tmp[:, 0, :], tmp[:, 0, :], 0.044715, 1.0, ALU.mult, ALU.add))
                nc.vector.tensor_tensor(tmp[:, 0, :], tmp[:, 0, :], bank[:, :], ALU.mult).then_inc(gu_done, 1)
                dve.wait_ge(gt_done, t + 1)
                nc.vector.scalar_tensor_tensor(gel[:, t, :], tmp[:, 0, :], 1.0, bank[:, :], ALU.add,
                                               ALU.mult).then_inc(gel_done, 1)

            def rec(t):
                dve.wait_ge(gel_done, t + 1)
                dve.wait_ge(scan_done, t + 1)
                if t:
                    dve.wait_ge(rec_ready, t)
                nc.vector.scalar_tensor_tensor(tmp[:, 1, :], xr[:, t, 3:3 + S], 0.5, gel[:, t, :],
                                               ALU.mult, ALU.mult).then_inc(rec_f_done, 1)
                dve.wait_ge(rec_hi_done, t + 1)
                nc.vector.tensor_tensor(mix_lo[:, 4 + t, :], tmp[:, 1, :], mix_hi[:, 4 + t, :].bitcast(F32),
                                        ALU.subtract).then_inc(rec_ready, 1)

            for hp in range(112):
                n = START[2] + hp // 2
                if hp >= 10 and hp % 2 == 0 and n < START[4] - 1:
                    cut_lo_n(n + 3)
                if hp == 80:
                    dve.wait_ge(scan_done, 4)
                    zero_yacc(KF)
                if hp >= 88 and hp % 8 == 0:
                    add_y(1, (hp - 80) // 8 - 1)
                for e, arg in EVENTS.get(hp, ()):
                    if e == "att":
                        att_step(arg)
                    elif e == "conv":
                        conv(arg)
                    elif e == "gate_a":
                        gate_a(arg)
                    elif e == "scan":
                        scan(arg)
                    elif e == "gelu":
                        gelu(arg)
                    elif e == "rec":
                        rec(arg)
            add_y(1, 3)
            inverse_rms(3)
            cut_lo_n(START[4] + 2)
            cut_lo_n(START[4] + 3)
            residual(1)
            inverse_rms(4)
            cut_all_h(2, START[4])
            ffn(1)
            inverse_rms(5)
            residual(2)
            for half in range(2):
                for t in (1, 3):
                    dve.wait_ge(out_tr, 4 * half + 4)
                    nc.vector.tensor_copy(o_st[:, t, half * 512:half * 512 + 512], ps[t + 4 * half][:, :])\
                        .then_inc(out_v, 1)


_INS = ["x", "c", "w_ada", "b_ada", "norm_gain", "ffn1_w_in", "ffn1_w_out", "mix_w_in", "conv_w", "conv_b",
        "lru_w_x", "lru_b_x", "lru_w_a", "lru_b_a", "lru_lambda", "mix_w_out", "ffn2_w_in", "ffn2_w_out"]


def kernel(**inputs):
    import numpy as _np
    import concourse.bacc as _bacc
    from concourse import mybir as _mybir
    from concourse.bass_utils import run_bass_kernel_spmd as _run

    nc = _bacc.Bacc("TRN2", target_bir_lowering=False, num_devices=1)
    arrays, args = {}, []
    for name in _INS:
        a = _np.ascontiguousarray(inputs[name])
        arrays[f"in_{name}"] = a
        ap = nc.dram_tensor(f"in_{name}", a.shape, _mybir.dt.from_np(a.dtype), kind="ExternalInput").ap()
        args.append(ap[0])
    out = nc.dram_tensor("out_y", (1, S, D), _mybir.dt.float32, kind="ExternalOutput").ap()
    build(nc, *args, out[0])
    r = _run(nc, [arrays], core_ids=[0])
    return r.results[0]["out_y"]
```

```python
from contextlib import ExitStack

import numpy as np
import concourse.bass as bass
from concourse import mybir

D, S, FF, P = 1024, 512, 2816, 128
KD, KF = D // P, FF // P
DA = DR = D // 2
HD, HEADS = 64, 8
NT = S // P
CT = DR // P
TAPS = 4
EPS = 1e-6
F32, F32R, I32 = mybir.dt.float32, mybir.dt.float32r, mybir.dt.int32
ALU, ACT = mybir.AluOpType, mybir.ActivationFunctionType
SLOTS = 4

PHASES = [("ffn_in", KF, KD // 2), ("ffn_out", KD // 2, KF // 2), ("mix_in", 10, KD // 2),
          ("mix_out", KD // 2, KD // 2), ("ffn_in", KF, KD // 2), ("ffn_out", KD // 2, KF // 2)]
START = [0]
for _, g_, c_ in PHASES:
    START.append(START[-1] + g_ * c_)
USES = [[0] * SLOTS]
for _, g_, c_ in PHASES:
    USES.append([USES[-1][s] + g_ * len(range(s, c_, SLOTS)) for s in range(SLOTS)])
MIX_ORDER = [0, 2, 4, 6, 1, 3, 5, 8, 7, 9]
AT = {g: i for i, g in enumerate(MIX_ORDER)}
OUT_FIRST = [(0, 2), (0, 0), (1, 2), (1, 0), (0, 1), (1, 1), (0, 3), (1, 3)]
OUT_ORDER = [2, 0, 1, 3]
ADA_PE = 1
Y_AT = [94, 96, 104]
T_LAG, PV_LAG = 2, 4

Y_STEPS = [0, 24, 48]
TURNS = [("x", 0), ("x", 1), ("y", 0), ("x", 2), ("y", 1), ("x", 3), ("y", 2), ("y", 3)]

NU = HEADS * NT


def back(ph, j):
    return (3, 3, 3, 7)[j] if j < 4 else 4


def locate(n):
    ph = max(i for i in range(6) if START[i] <= n)
    j = n - START[ph]
    g, c = divmod(j, PHASES[ph][2])
    slot = c % SLOTS
    behind_long = PHASES[ph][2] != 4 and g or PHASES[ph][2] == 4 and g == 0 and ph and PHASES[ph - 1][2] != 4
    b = back(ph, c) if behind_long else 4
    if ph in (0, 2, 4) and j < 8:
        g, c = j % 2, j // 2
    elif ph == 3:
        g, c = OUT_FIRST[j] if j < 8 else (g, OUT_ORDER[c])
    return ph, g, c, slot, b


def mixer_events():
    ev = {}

    def at(h, *e):
        ev.setdefault(h, []).append(e)

    at(14, "evac", 0)
    for gi in range(1, 10):
        at(8 * (gi + 1), "evac", gi)
    for half in range(2):
        a, b = 2 * half, 2 * half + 1
        h = 8 * (AT[4 + half] + 1)
        at(h + 1 + half, "vtr", a)
        at(h + 2 + half, "vtr", b)
        h = 8 * (AT[6 + half] + 1)
        at(h + 1, "conv", a)
        at(h + 3, "gate_x", a)
        at(h + 4, "conv", b)
        at(h + 5, "gate_a", a)
        at(h + 7, "gate_x", b)
        at(h + 6, "om", a)
        at(h + 9, "gate_a", b)
        at(h + 10, "om", b)
        at(h + 11 + half, "roots", half)
        at(h + 13 + half, "scan", a)
        at(h + 14 + half, "scan", b)
    h = 8 * (AT[8] + 1)
    for t, g_at, r_at in ((0, h + 1, h + 5), (1, h + 3, h + 7), (2, 80, 88), (3, 82, 89)):
        at(g_at, "gelu", t)
        at(g_at + 1, "gelu_t", t)
        at(r_at, "rec", t)
        at(r_at + 1, "rec_lo", t)
    first, last = 8 * (AT[4] + 1) + 3, 85
    for i in range(NU + PV_LAG):
        at(first + i * (last - first) // (NU + PV_LAG - 1), "att", i)
    return ev


EVENTS = mixer_events()


def build(nc, x, c, w_ada, b_ada, norm_gain, ffn1_w_in, ffn1_w_out, mix_w_in, conv_w, conv_b,
          lru_w_x, lru_b_x, lru_w_a, lru_b_a, lru_lambda, mix_w_out, ffn2_w_in, ffn2_w_out, out):
    ctx = ExitStack()
    with ctx:
        def sem(name):
            return ctx.enter_context(nc.semaphore(name))

        place = [-(-nc.sbuf_base // 32) * 32]

        def sb(name, shape, dt=F32, at=None):
            size = int(np.prod(shape[1:])) * 4
            off = place[0] if at is None else at
            if at is None:
                place[0] += -(-size // 32) * 32
            return nc.alloc_sbuf_tensor_at(name, shape, dt, offset=off)

        xT = sb("xT", [P, KD, S])
        h_hi_at = place[0]
        h_hi = sb("h_hi", [P, KD, S], F32R)
        h_lo_at = place[0]
        h_lo = sb("h_lo", [P, KD, S], F32R)
        y_at = place[0]
        y = sb("y", [P, KD, S])
        arena = place[0]
        hid_hi = sb("hid_hi", [P, KF, S], F32R)
        hid_lo = sb("hid_lo", [P, KF, S], F32R)
        arena_end = place[0]
        raw = sb("raw", [P, SLOTS, 512])
        w_hi = sb("w_hi", [P, SLOTS, 512], F32R)
        w_lo = sb("w_lo", [P, SLOTS, 512], F32R)
        ada_raw = sb("ada_raw", [P, SLOTS, 512])
        ada_acc = sb("ada_acc", [P, 2, 512])
        tmp = sb("tmp", [P, 3, S])
        hid_f = sb("hid_f", [P, S])
        yacc = hid_f
        sq = tmp
        diag_y = sb("diag_y", [P, NT, P])
        diag_x = hid_f.rearrange("p (t q) -> p t q", t=NT)
        rms = sb("rms", [P, 2, NT])
        x_ss = sb("x_ss", [P, NT])
        x_ss_new = sb("x_ss_new", [P, NT])
        gg = sb("gg", [P, 3, KD, 2])
        warm = sb("warm", [P, 1])
        ones = sb("ones", [P, P])
        ident = sb("ident", [P, P])
        mask = sb("mask", [P, S])
        wx = sb("wx", [P, CT, P])
        wa = sb("wa", [P, CT, P])
        cols_a = sb("cols_a", [P, 120])
        cols_b = sb("cols_b", [P, 40])
        silu_c = sb("silu_c", [P, 3, KD])
        mod = sb("mod", [P, 72])
        A = sb("A", [P, 3, KD])
        G = sb("G", [P, 3, KD])
        eps = sb("eps", [P, 1])
        half_b = sb("half_b", [P, 2, CT])
        sp = sb("sp", [P, 8, CT])
        neg_max = sb("neg_max", [P, 4, 1])
        den = sb("den", [P, 4, 1])
        rden = sb("rden", [P, 4, 1])
        assert place[0] <= nc.sbuf_usable_end, (place[0], nc.sbuf_usable_end)
        x_in = sb("x_in", [P, NT, D], at=y_at)
        att = sb("att", [P, 4, S], at=y_at)
        pT = sb("pT", [P, 4, S], at=y_at + 8192)
        qT = sb("qT", [P, 4, S], at=arena)
        kT = sb("kT", [P, 4, S], at=arena + 8192)
        v_nat = sb("v_nat", [P, NT, DA], at=arena + 16384)
        mix_hi = sb("mix_hi", [P, KD, S], F32R, at=arena + 24576)
        mix_lo = sb("mix_lo", [P, KD, S], F32R, at=arena + 40960)
        xr = sb("xr", [P, CT, S + 8], at=arena + 57344)
        gel = sb("gel", [P, CT, S], at=arena + 65664)
        lru = sb("lru", [P, 7, S], at=arena + 73856)
        vT = sb("vT", [P, 2, S], at=arena + 69760)
        gyacc = sb("gyacc", [P, 2, S], at=h_lo_at)
        xgy = sb("xgy", [P, 2, S], at=h_lo_at + 4096)
        x_out = sb("x_out", [P, NT, D], at=h_hi_at)
        y_out = sb("y_out", [P, NT, D], at=h_lo_at)
        ada0 = sb("ada0", [P, 4, KD, 512], at=arena)
        iot = sb("iot", [P, 3, S], I32, at=arena + 65536)
        cnt = sb("cnt", [P, 3, S], at=arena + 71680)
        rows_a = sb("rows_a", [120, P], at=arena + 77824)
        rows_b = sb("rows_b", [32, P], at=arena + 78336)
        rows_c = sb("rows_c", [KD, P], at=arena + 78848)
        assert arena + 73856 + 7 * 2048 <= arena_end
        xc = [lru[:, 0, :], lru[:, 1, :]]
        tx = [lru[:, 2, :], lru[:, 3, :]]
        aa = [lru[:, 4, :], lru[:, 5, :]]
        om = [lru[:, 6, :], hid_f[:, :]]

        ps = [ctx.enter_context(nc.psum_tensor(f"ps{i}", [P, 512], F32)) for i in range(8)]
        bank_stat, bank_r, bank_mod, bank_tr = ps[4], ps[5], ps[6], ps[7]
        bank_s, bank_g, bank_pt, bank_o = ps[4], ps[5], ps[6], ps[7]

        consts_in = sem("consts_in")
        c_in = sem("c_in")
        x_loaded = [sem(f"x_loaded{t}") for t in range(NT)]
        ada0_in = [[sem(f"ada0_in{q}_{j}") for j in range(4)] for q in range(4)]
        ada0_done = sem("ada0_done")
        mod0_sum = sem("mod0_sum")
        mod0_ready = sem("mod0_ready")
        c_tr = sem("c_tr")
        c_ready = sem("c_ready")
        diag_ready = sem("diag_ready")
        wbd_in = sem("wbd_in")
        wbd_zero = sem("wbd_zero")
        out_done = sem("out_done")
        raw_in = [sem(f"raw_in{s}") for s in range(SLOTS)]
        ada_in = [sem(f"ada_in{s}") for s in range(SLOTS)]
        pool_consts = sem("pool_consts")
        pool_iota = sem("pool_iota")
        hi_done = sem("hi_done")
        lo_done = sem("lo_done")
        chunk_used = sem("chunk_used")
        cols_tr = sem("cols_tr")
        cols_ready = sem("cols_ready")
        tanh_c = sem("tanh_c")
        lam_abs = sem("lam_abs")
        silu_c_ready = sem("silu_c_ready")
        ada_done = sem("ada_done")
        ada_col = sem("ada_col")
        x_summed = sem("x_summed")
        x_tr = sem("x_tr")
        x0_ready = sem("x0_ready")
        xt_ready = sem("xt_ready")
        ss_ready = sem("ss_ready")
        rms_ready = sem("rms_ready")
        rstd_ready = sem("rstd_ready")
        h_scaled = sem("h_scaled")
        h_hi_done = sem("h_hi_done")
        h_ready = sem("h_ready")
        tanh_done = sem("tanh_done")
        silu_done = sem("silu_done")
        hid_f_done = sem("hid_f_done")
        hid_hi_done = sem("hid_hi_done")
        hid_ready = sem("hid_ready")
        tile_done = sem("tile_done")
        ysq_done = sem("ysq_done")
        y_done = sem("y_done")
        y_step = sem("y_step")
        xgy_done = sem("xgy_done")
        g_ready = sem("g_ready")
        turned = sem("turned")
        ysum_done = sem("ysum_done")
        t_ready = sem("t_ready")
        out_tr = sem("out_tr")
        out_v = sem("out_v")
        dve_step = sem("dve_step")
        act_step = sem("act_step")
        mix_evac = sem("mix_evac")
        xr_zero = sem("xr_zero")
        v_tr = sem("v_tr")
        v_ready = sem("v_ready")
        s_done = sem("s_done")
        negs_done = sem("negs_done")
        exp_done = sem("exp_done")
        p_ready = sem("p_ready")
        pt_done = sem("pt_done")
        pt_ready = sem("pt_ready")
        pv_done = sem("pv_done")
        o_hi_done = sem("o_hi_done")
        o_lo_done = sem("o_lo_done")
        conv_done = sem("conv_done")
        gate_done = sem("gate_done")
        tx_done = sem("tx_done")
        lru_a_done = sem("lru_a_done")
        om_done = sem("om_done")
        sqrt_done = sem("sqrt_done")
        scan_done = sem("scan_done")
        gsq_done = sem("gsq_done")
        gu_done = sem("gu_done")
        gt_done = sem("gt_done")
        gel_done = sem("gel_done")
        rec_f_done = sem("rec_f_done")
        rec_hi_done = sem("rec_hi_done")
        rec_ready = sem("rec_ready")

        w_in = {0: ffn1_w_in, 4: ffn2_w_in}
        w_out = {1: ffn1_w_out, 3: mix_w_out, 5: ffn2_w_out}

        def chunk_source(ph, g, c):
            if ph in w_in:
                v = w_in[ph].rearrange("(k p) (u f) -> p k u f", p=P, u=2)
                return [v[:, 2 * c + kk, :, bass.ds(g * P, P)] for kk in range(2)]
            if ph == 2:
                v = mix_w_in.rearrange("(k p) f -> p k f", p=P)
                return [v[:, 2 * c:2 * c + 2, MIX_ORDER[g] * 256:MIX_ORDER[g] * 256 + 256]]
            v = w_out[ph].rearrange("(k p) f -> p k f", p=P)
            return [v[:, 2 * c:2 * c + 2, bass.ds(g * 256, 256)]]

        def filled(ph, g, c):
            s = c % SLOTS
            per_group = len(range(s, PHASES[ph][2], SLOTS))
            before = sum(2 * (USES[q + 1][s] - USES[q][s]) if q in w_in else USES[q + 1][s] - USES[q][s]
                         for q in range(ph))
            each = 2 if ph in w_in else 1
            return 16 * (before + each * (c // SLOTS + 1)) + 16 * each * per_group * g

        def number(ph, g, c):
            return START[ph] + PHASES[ph][2] * g + c

        block = ctx.enter_context(nc.Block())

        @block.sync
        def _(sp_):
            def load(ph, g, c, s, n, b):
                if not isinstance(n, int) or n - b >= 0:
                    sp_.wait_ge(lo_done, n - b + 1)
                for kk, src in enumerate(chunk_source(ph, g, c)):
                    if ph in w_in:
                        dst = raw[:, s, kk * 256:kk * 256 + 256].rearrange("p (u f) -> p u f", u=2)
                    else:
                        dst = raw[:, s, :].rearrange("p (k f) -> p k f", k=2)
                    sp_.dma_start(dst, src).then_inc(raw_in[s], 16)

            def load_n(n):
                ph, g, c, s, b = locate(n)
                load(ph, g, c, s, n, b)

            def load_group(ph, g):
                for c in range(4):
                    load(ph, g, c, c, number(ph, g, c), 4)

            ada_v = w_ada.rearrange("(k p) n -> p k n", p=P)

            def load_ada(col, k, a):
                if not isinstance(a, int) or a >= SLOTS:
                    sp_.wait_ge(ada_done, a - (SLOTS - 1))
                sp_.dma_start(ada_raw[:, k % SLOTS, :], ada_v[:, k, bass.ds(col * 512, 512)])\
                    .then_inc(ada_in[k % SLOTS], 16)

            sp_.dma_start(rows_c[:, :], c.rearrange("(k p) -> k p", p=P)).then_inc(c_in, 16)
            for t in range(NT):
                sp_.dma_start(x_in[:, t, :], x[t * P:(t + 1) * P, :]).then_inc(x_loaded[t], 16)
            ada0_v = w_ada.rearrange("(k p) (m n) -> p k m n", p=P, n=D)
            for q in range(4):
                for j in range(4):
                    for k in (2 * j, 2 * j + 1):
                        sp_.dma_start(ada0[:, q, k, :].rearrange("p (m n) -> p m n", m=2),
                                      ada0_v[:, k, 0:2, 256 * q:256 * q + 256]).then_inc(ada0_in[q][j], 16)
                if q == 0:
                    sp_.dma_start(rows_b[0:16, :], conv_w.rearrange("w (t p) -> (w t) p", p=P))\
                        .then_inc(consts_in, 16)
                    for i, v in enumerate((conv_b, lru_b_x, lru_b_a, lru_lambda)):
                        sp_.dma_start(rows_b[16 + 4 * i:20 + 4 * i, :], v.rearrange("(t p) -> t p", p=P))\
                            .then_inc(consts_in, 16)
                    sp_.dma_start(rows_a[0:72, :], b_ada.rearrange("(t p) -> t p", p=P)).then_inc(consts_in, 16)
                    sp_.dma_start(rows_a[72:120, :], norm_gain.rearrange("s (t p) -> (s t) p", p=P))\
                        .then_inc(consts_in, 16)
                if q < 2:
                    load_n(2 * q)
                    load_n(2 * q + 1)
            for n in range(4, 8):
                load_n(n)
            sp_.wait_ge(wbd_zero, 1)
            for w, dst in ((lru_w_x, wx), (lru_w_a, wa)):
                v = w.rearrange("(t b) i j -> b i t j", b=2)
                for b in range(2):
                    sp_.dma_start(dst[64 * b:64 * b + 64, :, 64 * b:64 * b + 64], v[b])\
                        .then_inc(wbd_in, 16)
            load_group(0, 2)
            for k in range(KD):
                load_ada(4, k, k)
            with sp_.Fori(0, 9) as i:
                for b in range(2):
                    load_group(0, 2 * i + (3 + b))
                    for k in range(4 * b, 4 * b + 4):
                        load_ada(5 + i, k, 8 * i + (8 + k))
            load_group(0, KF - 1)
            for k in range(KD):
                load_ada(14, k, 80 + k)
            for j in range(PHASES[1][1] * PHASES[1][2]):
                g, cc = divmod(j, KF // 2)
                if g < 3 and cc in (4, 7, 8):
                    for k in {4: (0, 1, 2, 3), 7: (4, 5), 8: (6, 7)}[cc]:
                        load_ada(15 + g, k, 8 * (11 + g) + k)
                load_n(START[1] + j)
            for n in range(START[2], START[4] + 12):
                load_n(n)
            with sp_.Fori(0, 9) as i:
                for b in range(2):
                    load_group(4, 2 * i + (3 + b))
            load_group(4, KF - 1)
            for n in range(START[5], START[6]):
                load_n(n)
            for t in range(NT):
                sp_.wait_ge(out_v, 2 * t + 2)
                sp_.dma_start(out[t * P:(t + 1) * P, :], x_out[:, t, :]).then_inc(out_done, 16)
            sp_.wait_ge(out_done, 16 * NT)

        @block.gpsimd
        def _(pool):
            nc.gpsimd.memset(ident[:], 0.0).then_inc(pool_consts, 1)
            pool.wait_ge(pool_consts, 1)
            nc.gpsimd.affine_select(out=ident[:], in_=ident[:], compare_op=ALU.not_equal, fill=1.0,
                                    base=0, pattern=[[-1, P]], channel_multiplier=1)\
                .then_inc(pool_consts, 1)
            nc.gpsimd.memset(ones[:], 1.0).then_inc(pool_consts, 1)
            nc.gpsimd.memset(eps[:], EPS).then_inc(pool_consts, 1)
            nc.gpsimd.iota(iot[:, 0, :], [[-1, S]], base=S - P, channel_multiplier=1)\
                .then_inc(pool_iota, 1)
            nc.gpsimd.memset(wx[:], 0.0)
            nc.gpsimd.memset(wa[:], 0.0).then_inc(wbd_zero, 1)

            def cut_lo_n(n):
                slot = locate(n)[3]
                pool.wait_ge(hi_done, n + 1)
                nc.gpsimd.tensor_tensor(w_lo[:, slot, :], raw[:, slot, :], w_hi[:, slot, :].bitcast(F32),
                                        ALU.subtract).then_inc(lo_done, 1)

            def add_x(s, k):
                pool.wait_ge(t_ready, 8 * s + k + 1)
                nc.gpsimd.tensor_tensor(xT[:, k, :], xT[:, k, :], y[:, k, :], ALU.add).then_inc(xt_ready, 1)

            for n in range(8):
                cut_lo_n(n)
            for s in range(2):
                n0 = START[2 * s + 2]
                if s == 0:
                    pool.wait_ge(lo_done, n0 + 2)
                else:
                    for n in range(START[2] + 8, n0 + 2):
                        cut_lo_n(n)
                cut_lo_n(n0 + 2)
                cut_lo_n(n0 + 3)
                for k in range(KD):
                    add_x(s, k)
                    if k >= 4:
                        cut_lo_n(n0 + k)

        @block.tensor
        def _(pe):
            def products(slot, kk, bank0, moving, start, stop):
                hi, lo = moving
                for b in range(2):
                    o = ps[bank0 + b][:, :]
                    col = kk * 256 + b * P
                    wh, wl = w_hi[:, slot, col:col + P], w_lo[:, slot, col:col + P]
                    nc.tensor.matmul(o, wh, hi, start=start, stop=False)
                    nc.tensor.matmul(o, wh, lo, start=False, stop=False)
                    last = nc.tensor.matmul(o, wl, hi, start=False, stop=stop)
                return last

            def last_chunk(n, slot, k0, hi, lo):
                pe.wait_ge(lo_done, n + 1)
                for b in range(2):
                    o = ps[2 + b][:, :]
                    for kk in range(2):
                        col = kk * 256 + b * P
                        wh, wl = w_hi[:, slot, col:col + P], w_lo[:, slot, col:col + P]
                        nc.tensor.matmul(o, wh, hi[:, k0 + kk, :], start=False, stop=False)
                        nc.tensor.matmul(o, wh, lo[:, k0 + kk, :], start=False, stop=False)
                        last = nc.tensor.matmul(o, wl, hi[:, k0 + kk, :], start=False, stop=kk == 1)
                    last.then_inc(tile_done if b == 0 else chunk_used, 1)

            def keep_warm(n):
                for _ in range(n):
                    nc.tensor.matmul(bank_mod[:, 384:512], ones[:, :], ident[:, :], start=True, stop=True)

            def over_h(n, slot, c, parity, h_tiles=None):
                pe.wait_ge(lo_done, n + 1)
                for kk in range(2):
                    k = 2 * c + kk
                    if h_tiles is not None:
                        pe.wait_ge(h_ready, h_tiles + k + 1)
                    last = products(slot, kk, 2 * parity, (h_hi[:, k, :], h_lo[:, k, :]), k == 0,
                                    k == KD - 1)
                last.then_inc(chunk_used, 1)

            def sum_mod(col, pieces):
                pe.wait_ge(ada_done, pieces)
                for j in range(4):
                    dst = bank_mod[:, bass.ds(4 * col + j, 1)]
                    last = nc.tensor.matmul(dst, ada_acc[:, 0, j * P:(j + 1) * P], ones[:, 0:1],
                                            start=True, stop=True)
                last.then_inc(ada_col, 1)

            def sum_tiles(s):
                parts = [yacc, gyacc[:, 0, :], gyacc[:, 1, :]] if s < 2 else [yacc]
                pe.wait_ge(y_step, Y_STEPS[s] + (24 if s < 2 else 6))
                for t in range(NT):
                    for q, part in enumerate(parts):
                        nc.tensor.matmul(bank_stat[:, 3 * t + q:3 * t + q + 1], part[:, t * P:(t + 1) * P],
                                         ones[:, 0:1], start=(t == 0 and q == 0), stop=False,
                                         skip_group_check=True)

            def sum_rest(s):
                for b in range(2):
                    m = KD - 2 + b
                    pe.wait_ge(ysq_done, 8 * s + m + 1)
                    for t in range(NT):
                        c0, w = 3 * t, 2 if s < 2 else 1
                        last = nc.tensor.matmul(bank_stat[:, c0:c0 + w], sq[:, b, t * P:(t + 1) * P],
                                                gg[:, s, m, 0:w], start=False, stop=b == 1,
                                                skip_group_check=True)
                    if s < 2:
                        pe.wait_ge(xgy_done, 2 * s + b + 1)
                        for t in range(NT):
                            last = nc.tensor.matmul(bank_stat[:, 3 * t + 2:3 * t + 3],
                                                    xgy[:, b, t * P:(t + 1) * P], ones[:, 0:1],
                                                    start=False, stop=b == 1, skip_group_check=True)
                last.then_inc(ysum_done, 1)

            def turn(i):
                what, r = TURNS[i]
                if what == "y":
                    pe.wait_ge(y_done, 16 + 2 * r + 2)
                if i:
                    pe.wait_ge(turned, 2 * i)
                src = xT if what == "x" else y
                for t in range(NT):
                    for b in range(2):
                        o = (t % 2) * 256 + b * P
                        last = nc.tensor.transpose(ps[6 + t // 2][:, o:o + P],
                                                   src[:, 2 * r + b, t * P:(t + 1) * P], ident[:, :])
                last.then_inc(out_tr, 1)

            def spread(j):
                pe.wait_ge(diag_ready, j + 1)
                bank = bank_tr if j in (2, 4) else bank_r
                nc.tensor.matmul(bank[:, :], ones[:, :], (diag_y if j % 2 else diag_x)[:, :, :],
                                 start=True, stop=True)\
                    .then_inc(rstd_ready, 1)

            def sum_mod0(q):
                bank = (bank_mod, bank_tr)[q % 2]
                if q == 0:
                    pe.wait_ge(silu_c_ready, 1)
                elif q == 1:
                    pe.wait_ge(cols_ready, 1)
                else:
                    pe.wait_ge(mod0_ready, q - 1)
                for k in range(KD - ADA_PE, KD):
                    if k % 2 == 0 or k == KD - ADA_PE:
                        pe.wait_ge(ada0_in[q][k // 2], 32)
                    for j in range(4):
                        nc.tensor.matmul(bank[:, j:j + 1], ada0[:, q, k, j * P:(j + 1) * P],
                                         silu_c[:, 2, k:k + 1], start=(k == KD - ADA_PE and j == 0),
                                         stop=False, skip_group_check=True)
                pe.wait_ge(ada0_done, q + 1)
                for j in range(4):
                    last = nc.tensor.matmul(bank[:, j:j + 1], ada_acc[:, q % 2, j * P:(j + 1) * P],
                                            ones[:, 0:1], start=False, stop=True, skip_group_check=True)
                last.then_inc(mod0_sum, 1)

            def ffn(f):
                ph = 4 * f
                n0 = START[ph]

                def group(g, parity):
                    pe.wait_ge(hid_f_done, g + (KF * f - 1))
                    for c in range(4):
                        over_h(4 * g + (n0 + c), c, c, parity)

                group(2, 0)
                if f == 0:
                    sum_mod(4, 8)
                with pe.Fori(0, 9) as i:
                    for b in range(2):
                        group(2 * i + (3 + b), 1 - b)
                    if f == 0:
                        sum_mod(5 + i, 8 * i + 16)
                group(KF - 1, 1)
                if f == 0:
                    sum_mod(14, 88)
                ph += 1
                n0 = START[ph]
                for g in range(4):
                    if g < 2:
                        pe.wait_ge(hid_f_done, KF * (f + 1) - 1 + g)
                    else:
                        pe.wait_ge(y_done, 16 * f + 2 * (g - 1))

                    def over_hid(n, c, slot, start=False, stop=False):
                        pe.wait_ge(lo_done, n + 1)
                        for kk in range(2):
                            k = 2 * c + kk
                            if g == 0:
                                pe.wait_ge(hid_ready, k + (KF * f + 1))
                            if isinstance(k, int):
                                moving = hid_hi[:, k, :], hid_lo[:, k, :]
                            else:
                                moving = hid_hi[:, bass.ds(k, 1), :], hid_lo[:, bass.ds(k, 1), :]
                            last = products(slot, kk, 2 * (g % 2), moving, start and kk == 0,
                                            stop and kk == 1)
                        last.then_inc(chunk_used, 1)

                    n = n0 + 11 * g
                    over_hid(n, 0, 0, start=True)
                    if f == 1 and g:
                        turn(2 * g - 1)
                    with pe.Fori(0, 2) as i:
                        for j in range(1, 5):
                            over_hid(4 * i + (n + j), 4 * i + j, j % SLOTS)
                    over_hid(n + 9, 9, 1)
                    if f == 1:
                        turn(2 * g)
                    if g == 3:
                        sum_tiles(2 * f)
                    if g < 3:
                        over_hid(n + 10, 10, 2, stop=True)
                    else:
                        last_chunk(n + 10, 2, KF - 2, hid_hi, hid_lo)
                    if f == 0 and g < 3:
                        sum_mod(15 + g, 96 + 8 * g)

            pe.wait_ge(pool_consts, 4)
            pe.wait_ge(c_in, 16)
            nc.tensor.transpose(bank_tr[:, 168:176], rows_c[:, :], ident[0:KD, 0:KD]).then_inc(c_tr, 1)
            keep_warm(12)
            for t in range(NT):
                pe.wait_ge(x_loaded[t], 16)
            for k in range(KD):
                if k >= 4:
                    pe.wait_ge(x0_ready, k - 3)
                for t in range(NT):
                    last = nc.tensor.transpose(ps[k % 4][:, t * P:(t + 1) * P],
                                               x_in[:, t, k * P:(k + 1) * P], ident[:, :])
                last.then_inc(x_tr, 1)
            pe.wait_ge(consts_in, 16 * 7)
            pe.wait_ge(c_ready, 1)
            nc.tensor.transpose(bank_tr[:, 0:120], rows_a[:, :], ident[0:120, 0:120])
            nc.tensor.transpose(bank_tr[:, 128:160], rows_b[:, :], ident[0:32, 0:32]).then_inc(cols_tr, 1)
            spread(0)
            sum_mod0(0)
            for q in range(4):
                if q < 3:
                    sum_mod0(q + 1)
                if q == 0:
                    pe.wait_ge(x0_ready, KD)
                for g in range(2):
                    over_h(2 * q + g, (2 * q + g) % SLOTS, q, g, 0)
            ffn(0)
            sum_rest(0)
            keep_warm(4)
            spread(1)
            spread(2)
            keep_warm(10)

            def vtr(t):
                pe.wait_ge(mix_evac, AT[4 + t // 2] + 1)
                if t == 2:
                    pe.wait_ge(lru_a_done, 2)
                elif t:
                    pe.wait_ge(v_ready, t)
                for j in range(NT):
                    last = nc.tensor.transpose(bank_g[:, j * P:(j + 1) * P], vT[:, t % 2, j * P:(j + 1) * P],
                                               ident[:, :])
                last.then_inc(v_tr, 1)

            def att_step(i):
                if i < NU:
                    h, qt = divmod(i, NT)
                    p, r = h // 2, HD * (h % 2)
                    if i:
                        pe.wait_ge(negs_done, i)
                    if h % 4 == 0 and qt == 0:
                        pe.wait_ge(mix_evac, AT[2 + h // 4] + 1)
                    nc.tensor.matmul(bank_s[:, 0:(qt + 1) * P], qT[r:r + HD, p, qt * P:(qt + 1) * P],
                                     kT[r:r + HD, p, 0:(qt + 1) * P], start=True, stop=True)\
                        .then_inc(s_done, 1)
                if 0 <= i - T_LAG < NU:
                    u = i - T_LAG
                    qt = u % NT
                    pe.wait_ge(p_ready, u + 1)
                    if u:
                        pe.wait_ge(pt_ready, u)
                    for j in range(qt + 1):
                        last = nc.tensor.transpose(bank_pt[:, j * P:(j + 1) * P],
                                                   att[:, u % 4, j * P:(j + 1) * P], ident[:, :])
                    last.then_inc(pt_done, 1)
                if i >= PV_LAG:
                    u = i - PV_LAG
                    h, qt = divmod(u, NT)
                    p, r = h // 2, HD * (h % 2)
                    pe.wait_ge(pt_ready, u + 1)
                    if u % 16 == 0:
                        pe.wait_ge(v_ready, 2 if u == 0 else 4)
                    if u and u % 8 == 0:
                        pe.wait_ge(o_lo_done, p)
                    for j in range(qt + 1):
                        last = nc.tensor.matmul(bank_o[r:r + HD, qt * P:(qt + 1) * P],
                                                v_nat[:, j, h * HD:(h + 1) * HD],
                                                pT[:, u % 4, j * P:(j + 1) * P],
                                                start=(j == 0), stop=(j == qt))
                    last.then_inc(pv_done, 1)

            def gate(t, w, n):
                pe.wait_ge(conv_done, t + 1)
                if n % 4 == 0:
                    pe.wait_ge(wbd_in, 64)
                    pe.wait_ge(v_ready, n // 2 + 2)
                elif n % 2:
                    pe.wait_ge(tx_done, n // 2 + 1)
                else:
                    pe.wait_ge(lru_a_done, n // 2)
                nc.tensor.matmul(bank_g[:, :], w[:, t, :], xc[t % 2], start=True, stop=True)\
                    .then_inc(gate_done, 1)

            for hp in range(112):
                n = START[2] + hp // 2
                ph, g, c, slot, _ = locate(n)
                if hp >= 110:
                    if hp == 110:
                        last_chunk(n, slot, 2 * c, mix_hi, mix_lo)
                    continue
                kk = hp % 2
                k = 2 * c + kk
                if kk == 0:
                    pe.wait_ge(lo_done, n + 1)
                if ph == 2:
                    if hp < 16:
                        pe.wait_ge(h_ready, 8 + k + 1)
                    elif k == 0:
                        pe.wait_ge(mix_evac, g - 1)
                    moving = h_hi[:, k, :], h_lo[:, k, :]
                    start, stop = k == 0, k == KD - 1
                else:
                    start, stop = c == OUT_ORDER[0] and kk == 0, c == OUT_ORDER[-1] and kk == 1
                    if start and g < 2:
                        pe.wait_ge(mix_evac, 9 + g)
                    elif start:
                        pe.wait_ge(y_done, 8 + 2 * (g - 1))
                    if g == 0:
                        if k < 4:
                            pe.wait_ge(o_lo_done, k + 1)
                        else:
                            pe.wait_ge(rec_ready, k - 3)
                    moving = mix_hi[:, k, :], mix_lo[:, k, :]
                last = products(slot, kk, 2 * (g % 2), moving, start, stop)
                if kk == 1:
                    last.then_inc(chunk_used, 1)
                for e, arg in EVENTS.get(hp, ()):
                    if e == "vtr":
                        vtr(arg)
                    elif e == "att":
                        att_step(arg)
                    elif e == "gate_x":
                        gate(arg, wx, 2 * arg)
                    elif e == "gate_a":
                        gate(arg, wa, 2 * arg + 1)
            sum_tiles(1)
            sum_rest(1)
            keep_warm(4)
            spread(3)
            spread(4)
            keep_warm(10)
            for n in range(START[4], START[4] + 8):
                ph, g, c, slot, _ = locate(n)
                over_h(n, slot, c, g, 16)
            ffn(1)
            sum_rest(2)
            turn(7)

        @block.scalar
        def _(act):
            def cut(s, n, b, loaded):
                act.wait_ge(raw_in[s], loaded)
                if not isinstance(n, int) or n - b >= 0:
                    act.wait_ge(chunk_used, n - b + 1)
                nc.scalar.activation(w_hi[:, s, :], raw[:, s, :], ACT.Copy).then_inc(hi_done, 1)

            def cut_hi_n(n):
                ph, _, _, s, b = locate(n)
                g, j = divmod(n - START[ph], PHASES[ph][2])
                cut(s, n, b, filled(ph, g, j))

            def cut_hi_group(ph, g, chunks=range(4)):
                for c in chunks:
                    cut(c, number(ph, g, c), 4, filled(ph, g, c))

            def root(j, src, wait_sem, value):
                act.wait_ge(wait_sem, value)
                nc.scalar.activation(rms[:, j % 2, :], src, ACT.Sqrt, bias=eps[:, 0:1],
                                     scale=1.0 / D).then_inc(rms_ready, 1)

            y_ss = bank_stat[:, 0:3 * NT].rearrange("p (t q) -> p t q", q=3)[:, :, 0]

            def turn(i):
                what, r = TURNS[i]
                act.wait_ge(out_tr, i + 1)
                dst = x_out if what == "x" else y_out
                for u in range(2):
                    nc.scalar.activation(dst[:, 2 * u:2 * u + 2, 256 * r:256 * r + 256],
                                         ps[6 + u][:, :].rearrange("p (t f) -> p t f", t=2), ACT.Copy)\
                        .then_inc(turned, 1)

            def cut_h(s, k):
                act.wait_ge(h_scaled, 8 * s + k + 1)
                m = 24 * s + k
                nc.scalar.activation(h_hi[:, k, :], tmp[:, k % 3, :], ACT.Identity,
                                     bias=mod[:, m:m + 1]).then_inc(h_hi_done, 1)

            def cut_all_h(s, n0):
                for k in range(KD):
                    if k >= 4:
                        cut_hi_n(n0 + k)
                    cut_h(s, k)

            def swiglu(f, g, parity, first):
                ahead = 7 if isinstance(g, int) and g == 0 else 4
                act.wait_ge(chunk_used, 4 * g + (START[4 * f] + ahead))
                if not first:
                    act.wait_ge(hid_f_done, KF * f + g)
                nc.scalar.activation(tmp[:, 0, :], ps[2 * parity][:, :], ACT.Tanh, scale=0.5)\
                    .then_inc(tanh_done, 1)
                act.wait_ge(hid_f_done, KF * f + g + 1)
                dst = hid_hi[:, g, :] if isinstance(g, int) else hid_hi[:, bass.ds(g, 1), :]
                src = hid_f[:, :] if isinstance(g, int) else hid_f[:, :].rearrange("p (o s) -> p o s", o=1)
                nc.scalar.activation(dst, src, ACT.Copy).then_inc(hid_hi_done, 1)

            def take_y(s, ph, g):
                if g == 3:
                    act.wait_ge(tile_done, s + 1)
                else:
                    act.wait_ge(chunk_used, START[3] + 7 if (ph, g) == (3, 0) else
                                number(ph, g, PHASES[ph][2] - 1) + 1)
                if g == 0:
                    act.wait_ge(g_ready, s + 1)

                def square(m):
                    if m >= 2:
                        act.wait_ge(y_step, Y_STEPS[s] + (4 * (m - 2) + 2 if s < 2 else m - 1))
                    nc.scalar.activation(sq[:, m % 2, :], ps[2 * (g % 2) + m % 2][:, :], ACT.Square)\
                        .then_inc(ysq_done, 1)

                def scale(m):
                    nc.scalar.activation(y[:, m, :], ps[2 * (g % 2) + m % 2][:, :], ACT.Identity,
                                         scale=G[:, s, m:m + 1]).then_inc(y_done, 1)

                if g < 3:
                    square(2 * g)
                    square(2 * g + 1)
                    scale(2 * g)
                    scale(2 * g + 1)
                else:
                    square(6)
                    scale(6)
                    act.wait_ge(chunk_used, START[ph + 1])
                    square(7)
                    scale(7)

            def load_root_table():
                nc.scalar.activation(warm[:, :], eps[:, :], ACT.Sqrt)

            def ffn(f):
                ph = 4 * f
                cut_hi_group(ph, 2, range(3))
                swiglu(f, 0, 0, f == 0)
                cut_hi_group(ph, 2, range(3, 4))
                swiglu(f, 1, 1, False)
                with act.Fori(0, 9) as i:
                    for b in range(2):
                        cut_hi_group(ph, 2 * i + (3 + b))
                        swiglu(f, 2 * i + (2 + b), b, False)
                cut_hi_group(ph, KF - 1)
                swiglu(f, KF - 2, 0, False)
                ph += 1
                for j in range(PHASES[ph][1] * PHASES[ph][2]):
                    g, c = divmod(j, KF // 2)
                    cut_hi_n(START[ph] + j)
                    if f == 1 and c == 1 and g:
                        turn(2 * g - 2)
                    if f == 1 and c == 3 and g:
                        turn(2 * g - 1)
                    if c == 3:
                        if g == 0:
                            swiglu(f, KF - 1, 1, False)
                            load_root_table()
                        else:
                            take_y(2 * f, ph, g - 1)
                if f == 0:
                    cut_hi_n(START[2])
                    cut_hi_n(START[2] + 1)
                else:
                    turn(6)
                take_y(2 * f, ph, 3)

            act.wait_ge(c_ready, 1)
            nc.scalar.activation(silu_c[:, 0, :], silu_c[:, 1, :], ACT.Tanh, scale=0.5).then_inc(tanh_c, 1)
            for t in range(NT):
                act.wait_ge(x_loaded[t], 16)
                nc.scalar.activation(h_lo[:, 2 * t:2 * t + 2, :].rearrange("p k s -> p (k s)"),
                                     x_in[:, t, :], ACT.Square, accum_out=x_ss[:, t:t + 1])\
                    .then_inc(x_summed, 1)
            act.wait_ge(x_summed, NT)
            nc.scalar.activation(rms[:, 0, :], x_ss[:, :], ACT.Sqrt, bias=eps[:, 0:1], scale=1.0 / D)\
                .then_inc(rms_ready, 1)
            for k in range(KD):
                act.wait_ge(x_tr, k + 1)
                nc.scalar.activation(xT[:, k, :], ps[k % 4][:, :], ACT.Copy).then_inc(x0_ready, 1)
            act.wait_ge(lam_abs, 1)
            nc.scalar.activation(sp[:, 1, :], sp[:, 0, :], ACT.Exp, scale=-1.0).then_inc(tanh_c, 1)
            for q in range(4):
                cut_hi_n(2 * q)
                cut_hi_n(2 * q + 1)
                act.wait_ge(mod0_ready, q + 1)
                cut_h(0, 2 * q)
                cut_h(0, 2 * q + 1)
            ffn(0)

            cut_hi_n(START[2] + 2)
            cut_hi_n(START[2] + 3)
            root(1, y_ss, ysum_done, 1)
            root(2, x_ss[:, :], ss_ready, 1)
            cut_all_h(1, START[2])

            def evac(gi):
                grp = MIX_ORDER[gi]
                act.wait_ge(chunk_used, START[2] + (7 if gi == 0 else 4 * gi + 4))
                if grp == 6:
                    act.wait_ge(xr_zero, 1)
                if grp in (5, 9):
                    act.wait_ge(v_tr, 2 if grp == 5 else 4)
                for b in range(2):
                    t = 2 * (grp % 2) + b if grp // 2 != 2 else b
                    src = ps[2 * (gi % 2) + b][:, :]
                    if grp < 6:
                        dst = (qT, kT, vT)[grp // 2][:, t, :]
                    elif grp < 8:
                        dst = xr[:, t, 3:3 + S]
                    else:
                        dst = gel[:, t, :]
                    last = nc.scalar.activation(dst, src, ACT.Copy)
                last.then_inc(mix_evac, 1)

            def vtr(t):
                act.wait_ge(v_tr, t + 1)
                nc.scalar.activation(v_nat[:, :, t * P:(t + 1) * P],
                                     bank_g[:, :].rearrange("p (j f) -> p j f", j=NT), ACT.Copy)\
                    .then_inc(v_ready, 1)

            def att_step(i):
                if i < NU:
                    w = (i % NT + 1) * P
                    act.wait_ge(negs_done, i + 1)
                    nc.scalar.activation(att[:, i % 4, 0:w], att[:, i % 4, 0:w], ACT.Exp,
                                         bias=neg_max[:, i % 4, :], scale=-1.0,
                                         accum_out=den[:, i % 4, :]).then_inc(exp_done, 1)
                if 0 <= i - T_LAG < NU:
                    u = i - T_LAG
                    w = (u % NT + 1) * P
                    act.wait_ge(pt_done, u + 1)
                    if u >= 4:
                        act.wait_ge(pv_done, u - 3)
                    nc.scalar.activation(pT[:, u % 4, 0:w], bank_pt[:, 0:w], ACT.Copy).then_inc(pt_ready, 1)
                if i % 8 == (7 + PV_LAG) % 8 and i >= 7 + PV_LAG:
                    p = (i - 7 - PV_LAG) // 8
                    act.wait_ge(pv_done, 8 * p + 8)
                    nc.scalar.activation(mix_hi[:, p, :], bank_o[:, :], ACT.Copy).then_inc(o_hi_done, 1)

            def gate_x(t):
                act.wait_ge(gate_done, 2 * t + 1)
                if t >= 2:
                    act.wait_ge(scan_done, t - 1)
                nc.scalar.activation(tx[t % 2], bank_g[:, :], ACT.Tanh, bias=half_b[:, 0, t:t + 1],
                                     scale=0.5).then_inc(tx_done, 1)

            def gate_a(t):
                act.wait_ge(gate_done, 2 * t + 2)
                if t:
                    act.wait_ge(om_done, t)
                else:
                    act.wait_ge(h_ready, 16)
                nc.scalar.activation(tmp[:, 0, :], bank_g[:, :], ACT.Tanh, bias=half_b[:, 1, t:t + 1],
                                     scale=0.5).then_inc(act_step, 1)
                act.wait_ge(act_step, t + 1)
                nc.scalar.activation(tmp[:, 1, :], tmp[:, 0, :], ACT.Tanh, bias=sp[:, 6, t:t + 1],
                                     scale=sp[:, 6, t:t + 1])
                nc.scalar.activation(aa[t % 2], tmp[:, 0, :], ACT.Exp, bias=sp[:, 7, t:t + 1],
                                     scale=sp[:, 7, t:t + 1]).then_inc(lru_a_done, 1)

            def roots(pair):
                act.wait_ge(om_done, 2 * pair + 2)
                for b in range(2):
                    nc.scalar.activation(om[b], om[b], ACT.Sqrt).then_inc(sqrt_done, 1)

            def gelu(t):
                act.wait_ge(mix_evac, AT[8 + t // 2] + 1)
                if t:
                    act.wait_ge(gel_done, t)
                nc.scalar.activation(tmp[:, 2, :], gel[:, t, :], ACT.Square).then_inc(gsq_done, 1)

            def gelu_t(t):
                act.wait_ge(gu_done, t + 1)
                nc.scalar.activation(tmp[:, 2, :], tmp[:, 2, :], ACT.Tanh,
                                     scale=float(np.sqrt(2 / np.pi))).then_inc(gt_done, 1)

            def rec(t):
                act.wait_ge(rec_f_done, t + 1)
                nc.scalar.activation(mix_hi[:, 4 + t, :], gel[:, t, :], ACT.Copy).then_inc(rec_hi_done, 1)

            def run_events(hp):
                for e, arg in EVENTS.get(hp, ()):
                    if e == "evac":
                        evac(arg)
                    elif e == "vtr":
                        vtr(arg)
                    elif e == "att":
                        att_step(arg)
                    elif e == "gate_x":
                        gate_x(arg)
                    elif e == "gate_a":
                        gate_a(arg)
                    elif e == "roots":
                        roots(arg)
                    elif e == "gelu":
                        gelu(arg)
                    elif e == "gelu_t":
                        gelu_t(arg)
                    elif e == "rec":
                        rec(arg)

            for hp in range(112):
                n = START[2] + hp // 2
                if hp >= 10 and hp % 2 == 0 and n < START[4] - 1:
                    cut_hi_n(n + 3)
                if hp == 90:
                    load_root_table()
                if hp in Y_AT:
                    take_y(1, 3, Y_AT.index(hp))
                run_events(hp)
            take_y(1, 3, 3)
            cut_hi_n(START[4] + 2)
            cut_hi_n(START[4] + 3)
            root(3, y_ss, ysum_done, 2)
            root(4, x_ss[:, :], ss_ready, 2)
            cut_all_h(2, START[4])
            ffn(1)
            root(5, y_ss, ysum_done, 3)

        @block.vector
        def _(dve):
            steps = [0]

            def link(ins):
                steps[0] += 1
                ins.then_inc(dve_step, 1)
                dve.wait_ge(dve_step, steps[0])

            def cut(s, n):
                dve.wait_ge(hi_done, n + 1)
                nc.vector.tensor_tensor(w_lo[:, s, :], raw[:, s, :], w_hi[:, s, :].bitcast(F32),
                                        ALU.subtract).then_inc(lo_done, 1)

            def cut_lo_n(n):
                cut(locate(n)[3], n)

            def cut_lo_group(ph, g, chunks=range(4)):
                for c in chunks:
                    cut(c, number(ph, g, c))

            def ada(col, k, a):
                s = k % SLOTS
                dve.wait_ge(ada_in[s], 32 * (col - 4) + 16 * (k // SLOTS + 1))
                acc = ada_acc[:, 0, :]
                if k == 0:
                    if not isinstance(col, int) or col > 4:
                        dve.wait_ge(ada_col, col - 4)
                    nc.vector.tensor_scalar(acc, ada_raw[:, s, :], silu_c[:, 2, 0:1], None, ALU.mult)\
                        .then_inc(ada_done, 1)
                else:
                    dve.wait_ge(ada_done, a)
                    nc.vector.scalar_tensor_tensor(acc, ada_raw[:, s, :], silu_c[:, 2, k:k + 1], acc,
                                                   ALU.mult, ALU.add).then_inc(ada_done, 1)

            def finish_mod(lo, hi, count):
                dve.wait_ge(ada_col, count)
                link(nc.vector.tensor_tensor(mod[:, lo:hi], bank_mod[:, lo:hi], cols_a[:, lo:hi], ALU.add))

            def make_a(s):
                return nc.vector.scalar_tensor_tensor(A[:, s, :], mod[:, 24 * s + 8:24 * s + 16], 1.0,
                                                      cols_a[:, 72 + 16 * s:80 + 16 * s], ALU.add, ALU.mult)

            def make_g(s):
                link(nc.vector.scalar_tensor_tensor(G[:, s, :], mod[:, 24 * s + 16:24 * s + 24], 1.0,
                                                    cols_a[:, 80 + 16 * s:88 + 16 * s], ALU.add, ALU.mult))
                if s != 1:
                    link(nc.vector.tensor_scalar(G[:, s, :], G[:, s, :], 0.5, None, ALU.mult))
                nc.vector.tensor_tensor(gg[:, s, :, 1], G[:, s, :], G[:, s, :], ALU.mult)\
                    .then_inc(g_ready, 1)

            def invert_rms(j):
                dve.wait_ge(rms_ready, j + 1)
                link(nc.vector.reciprocal(rms[:, j % 2, :], rms[:, j % 2, :]))

            def make_diag(j):
                diag = diag_y if j % 2 else diag_x
                for t in range(NT):
                    last = nc.vector.tensor_scalar(diag[:, t, :], ident[:, :], rms[:, j % 2, t:t + 1], None,
                                                   ALU.mult)
                last.then_inc(diag_ready, 1)

            def scale_h(s, k):
                if k >= 3:
                    dve.wait_ge(h_ready, 8 * s + k - 2)
                bank = bank_tr if s else bank_r
                nc.vector.scalar_tensor_tensor(tmp[:, k % 3, :], xT[:, k, :], A[:, s, k:k + 1],
                                               bank[:, :], ALU.mult, ALU.mult).then_inc(h_scaled, 1)

            def rest_h(s, k):
                dve.wait_ge(h_hi_done, 8 * s + k + 1)
                m = 24 * s + k
                nc.vector.scalar_tensor_tensor(h_lo[:, k, :], tmp[:, k % 3, :], mod[:, m:m + 1],
                                               h_hi[:, k, :].bitcast(F32), ALU.add,
                                               ALU.subtract).then_inc(h_ready, 1)

            def next_h(s, n0):
                invert_rms(2 * s + 1)
                r = rms[:, 1, :]
                stat = bank_stat[:, 0:3 * NT].rearrange("p (t q) -> p t q", q=3)
                new = x_ss_new[:, :]
                link(nc.vector.tensor_tensor(new, stat[:, :, 1], r, ALU.mult))
                link(nc.vector.scalar_tensor_tensor(new, stat[:, :, 2], 2.0, new, ALU.mult, ALU.add))
                link(nc.vector.tensor_tensor(new, new, r, ALU.mult))
                link(nc.vector.tensor_tensor(new, new, x_ss[:, :], ALU.add))
                nc.vector.tensor_scalar(x_ss[:, :], new, 0.0, None, ALU.max).then_inc(ss_ready, 1)
                make_diag(2 * s + 1)
                invert_rms(2 * s + 2)
                make_diag(2 * s + 2)

                def scale_y(k):
                    nc.vector.tensor_tensor(y[:, k, :], y[:, k, :], bank_r[:, :], ALU.mult)\
                        .then_inc(t_ready, 1)

                dve.wait_ge(rstd_ready, 2 * s + 2)
                scale_y(0)
                scale_y(1)
                for k in range(KD + 1):
                    if k < KD:
                        if k == 0:
                            dve.wait_ge(rstd_ready, 2 * s + 3)
                        dve.wait_ge(xt_ready, 8 * s + k + 1)
                        scale_h(s + 1, k)
                    if k != 1:
                        rest_h(s + 1, max(k - 1, 0))
                    if k + 2 < KD:
                        scale_y(k + 2)

            def silu_up(f, g, parity):
                dve.wait_ge(tanh_done, KF * f + g + 1)
                nc.vector.scalar_tensor_tensor(tmp[:, 1, :], tmp[:, 0, :], 1.0, ps[2 * parity][:, :],
                                               ALU.add, ALU.mult).then_inc(silu_done, 1)
                dve.wait_ge(silu_done, KF * f + g + 1)
                if not isinstance(g, int) or g:
                    dve.wait_ge(hid_ready, KF * f + g)
                nc.vector.scalar_tensor_tensor(hid_f[:, :], tmp[:, 1, :], 0.5, ps[2 * parity + 1][:, :],
                                               ALU.mult, ALU.mult).then_inc(hid_f_done, 1)

            def cut_hid(f, g):
                dve.wait_ge(hid_hi_done, KF * f + g + 1)
                if isinstance(g, int):
                    o, i0, i1 = hid_lo[:, g, :], hid_f[:, :], hid_hi[:, g, :].bitcast(F32)
                else:
                    o, i1 = hid_lo[:, bass.ds(g, 1), :], hid_hi[:, bass.ds(g, 1), :].bitcast(F32)
                    i0 = hid_f[:, :].rearrange("p (o s) -> p o s", o=1)
                nc.vector.tensor_tensor(o, i0, i1, ALU.subtract).then_inc(hid_ready, 1)

            def add_y(s, g):
                for b in range(2):
                    m = 2 * g + b
                    if m < 6:
                        dve.wait_ge(ysq_done, 8 * s + m + 1)
                    if m == 0:
                        dve.wait_ge(g_ready, s + 1)
                    n = Y_STEPS[s] + (4 if s < 2 else 1) * min(m, 6)
                    if m:
                        dve.wait_ge(y_step, n)
                    if m == 0:
                        nc.vector.tensor_scalar(yacc[:, :], sq[:, b, :], 1.0, None, ALU.mult)\
                            .then_inc(y_step, 1)
                    elif m < 6:
                        nc.vector.tensor_tensor(yacc[:, :], yacc[:, :], sq[:, b, :], ALU.add)\
                            .then_inc(y_step, 1)
                    if s == 2:
                        continue
                    if m == 0:
                        nc.vector.tensor_scalar(gyacc[:, 0, :], sq[:, b, :], gg[:, s, m, 1:2], None,
                                                ALU.mult).then_inc(y_step, 1)
                    elif m < 6:
                        nc.vector.scalar_tensor_tensor(gyacc[:, 0, :], sq[:, b, :], gg[:, s, m, 1:2],
                                                       gyacc[:, 0, :], ALU.mult, ALU.add)\
                            .then_inc(y_step, 1)
                    dve.wait_ge(y_done, 8 * s + m + 1)
                    nc.vector.tensor_tensor(xgy[:, b, :], xT[:, m, :], y[:, m, :], ALU.mult)\
                        .then_inc(y_step if m < 6 else xgy_done, 1)
                    if m < 6:
                        dve.wait_ge(y_step, n + 3)
                        if m == 0:
                            nc.vector.tensor_copy(gyacc[:, 1, :], xgy[:, b, :]).then_inc(y_step, 1)
                        else:
                            nc.vector.tensor_tensor(gyacc[:, 1, :], gyacc[:, 1, :], xgy[:, b, :], ALU.add)\
                                .then_inc(y_step, 1)

            def ffn(f):
                ph = 4 * f
                dve.wait_ge(lo_done, START[ph] + 8)
                cut_lo_group(ph, 2, range(3))
                silu_up(f, 0, 0)
                cut_hid(f, 0)
                cut_lo_group(ph, 2, range(3, 4))
                silu_up(f, 1, 1)
                cut_hid(f, 1)
                if f == 0:
                    for k in range(KD):
                        ada(4, k, k)
                with dve.Fori(0, 9) as i:
                    for b in range(2):
                        g = 2 * i + (2 + b)
                        cut_lo_group(ph, g + 1)
                        if f == 0:
                            for k in (4 * b, 4 * b + 1):
                                ada(5 + i, k, 8 * i + (8 + k))
                        silu_up(f, g, b)
                        if f == 0:
                            for k in (4 * b + 2, 4 * b + 3):
                                ada(5 + i, k, 8 * i + (8 + k))
                        cut_hid(f, g)
                cut_lo_group(ph, KF - 1)
                silu_up(f, KF - 2, 0)
                cut_hid(f, KF - 2)
                if f == 0:
                    for k in range(KD):
                        ada(14, k, 80 + k)
                ph += 1
                for j in range(PHASES[ph][1] * PHASES[ph][2]):
                    g, c = divmod(j, KF // 2)
                    cut_lo_n(START[ph] + j)
                    if c == 3:
                        if g == 0:
                            silu_up(f, KF - 1, 1)
                            cut_hid(f, KF - 1)
                            dve.wait_ge(hid_ready, KF * (f + 1))
                            if f == 0:
                                finish_mod(16, 48, 11)
                                make_g(0)
                                make_g(1)
                                link(make_a(1))
                        else:
                            add_y(2 * f, g - 1)
                    if f == 0 and g < 3 and 4 <= c < 8:
                        for k in (2 * c - 8, 2 * c - 7):
                            ada(15 + g, k, 8 * (11 + g) + k)
                if f == 0:
                    cut_lo_n(START[2])
                    cut_lo_n(START[2] + 1)
                if f == 0:
                    add_y(0, 3)

            link(nc.vector.memset(gg[:, :, :, 0], 1.0))
            dve.wait_ge(c_tr, 1)
            nc.vector.tensor_copy(silu_c[:, 1, :], bank_tr[:, 168:176]).then_inc(c_ready, 1)
            dve.wait_ge(tanh_c, 1)
            link(nc.vector.scalar_tensor_tensor(silu_c[:, 0, :], silu_c[:, 0, :], 1.0, silu_c[:, 1, :],
                                                ALU.add, ALU.mult))
            nc.vector.tensor_scalar(silu_c[:, 2, :], silu_c[:, 0, :], 0.5, None, ALU.mult)\
                .then_inc(silu_c_ready, 1)
            dve.wait_ge(silu_c_ready, 1)

            def softplus():
                dve.wait_ge(tanh_c, 2)
                link(nc.vector.tensor_scalar(sp[:, 3, :], sp[:, 1, :], 2.0, None, ALU.add))
                link(nc.vector.reciprocal(sp[:, 3, :], sp[:, 3, :]))
                link(nc.vector.tensor_tensor(sp[:, 3, :], sp[:, 3, :], sp[:, 1, :], ALU.mult))
                link(nc.vector.tensor_tensor(sp[:, 4, :], sp[:, 3, :], sp[:, 3, :], ALU.mult))
                link(nc.vector.memset(sp[:, 5, :], 1.0 / 17))
                for n in (15, 13, 11, 9, 7, 5, 3, 1):
                    link(nc.vector.tensor_tensor(sp[:, 5, :], sp[:, 5, :], sp[:, 4, :], ALU.mult))
                    link(nc.vector.tensor_scalar(sp[:, 5, :], sp[:, 5, :], 1.0 / n, None, ALU.add))
                link(nc.vector.tensor_tensor(sp[:, 5, :], sp[:, 5, :], sp[:, 3, :], ALU.mult))
                link(nc.vector.tensor_scalar(sp[:, 2, :], sp[:, 2, :], 0.0, 0.5, ALU.max, ALU.mult))
                link(nc.vector.tensor_tensor(sp[:, 5, :], sp[:, 5, :], sp[:, 2, :], ALU.add))
                link(nc.vector.tensor_scalar(sp[:, 6, :], sp[:, 5, :], 8.0, None, ALU.mult))
                link(nc.vector.tensor_scalar(sp[:, 7, :], sp[:, 5, :], -8.0, None, ALU.mult))
                link(nc.vector.tensor_scalar(half_b[:, 0, :], cols_b[:, 28:32], 0.5, None, ALU.mult))
                link(nc.vector.tensor_scalar(half_b[:, 1, :], cols_b[:, 32:36], 0.5, None, ALU.mult))

            def make_mask():
                dve.wait_ge(pool_iota, 1)
                for n, bits in ((1, 3), (2, 15)):
                    link(nc.vector.tensor_scalar(iot[:, n, :], iot[:, 0, :], bits, None, ALU.bitwise_and))
                link(nc.vector.tensor_copy(cnt[:, 0, :], iot[:, 0, :]))
                link(nc.vector.tensor_scalar(cnt[:, 1, :], cnt[:, 0, :], 128.0, None, ALU.is_le))
                for n in (1, 2):
                    link(nc.vector.tensor_copy(cnt[:, 2, :], iot[:, n, :]))
                    link(nc.vector.scalar_tensor_tensor(cnt[:, 1, :], cnt[:, 2, :], 0.0, cnt[:, 1, :],
                                                        ALU.is_equal, ALU.add))
                link(nc.vector.scalar_tensor_tensor(cnt[:, 1, :], cnt[:, 0, :], 0.0, cnt[:, 1, :],
                                                    ALU.is_ge, ALU.mult))
                link(nc.vector.tensor_scalar(mask[:, :], cnt[:, 1, :], 0.0, -8e30, ALU.is_equal, ALU.mult))
                for n in (2, 3):
                    link(nc.vector.tensor_scalar(cnt[:, 2, :], cnt[:, 1, :], float(n), float(8 * np.log(n)),
                                                 ALU.is_equal, ALU.mult))
                    link(nc.vector.tensor_tensor(mask[:, :], mask[:, :], cnt[:, 2, :], ALU.add))

            def ada0_quarter(q):
                acc = ada_acc[:, q % 2, :]
                if q >= 2:
                    dve.wait_ge(mod0_sum, q - 1)
                for k in range(KD - ADA_PE):
                    if k % 2 == 0:
                        dve.wait_ge(ada0_in[q][k // 2], 32)
                    if k == 0:
                        last = nc.vector.tensor_scalar(acc, ada0[:, q, k, :], silu_c[:, 2, 0:1], None,
                                                       ALU.mult)
                    else:
                        last = nc.vector.scalar_tensor_tensor(acc, ada0[:, q, k, :], silu_c[:, 2, k:k + 1],
                                                              acc, ALU.mult, ALU.add)
                    if k < KD - ADA_PE - 1:
                        link(last)
                last.then_inc(ada0_done, 1)

            def mod0_quarter(q):
                bank = (bank_mod, bank_tr)[q % 2]
                dve.wait_ge(mod0_sum, q + 1)
                two = lambda v: v.rearrange("p (m k) -> p m k", m=2)[:, :, 2 * q:2 * q + 2]
                link(nc.vector.tensor_tensor(two(mod[:, 0:16]), bank[:, 0:4].rearrange("p (m k) -> p m k", m=2),
                                             two(cols_a[:, 0:16]), ALU.add))
                k = 2 * q
                nc.vector.scalar_tensor_tensor(A[:, 0, k:k + 2], mod[:, 8 + k:10 + k], 1.0,
                                               cols_a[:, 72 + k:74 + k], ALU.add, ALU.mult)\
                    .then_inc(mod0_ready, 1)
                dve.wait_ge(mod0_ready, q + 1)

            make_mask()
            invert_rms(0)
            make_diag(0)
            ada0_quarter(0)
            dve.wait_ge(cols_tr, 1)
            link(nc.vector.tensor_copy(cols_b[:, 8:40], bank_tr[:, 128:160]))
            nc.vector.tensor_copy(cols_a[:, :], bank_tr[:, 0:120]).then_inc(cols_ready, 1)
            dve.wait_ge(cols_ready, 1)
            lam = cols_b[:, 36:40]
            link(nc.vector.tensor_scalar(sp[:, 2, :], lam, -1.0, None, ALU.mult))
            nc.vector.tensor_tensor(sp[:, 0, :], sp[:, 2, :], lam, ALU.max).then_inc(lam_abs, 1)
            for q in range(4):
                if q < 3:
                    ada0_quarter(q + 1)
                mod0_quarter(q)
                if q == 0:
                    dve.wait_ge(rstd_ready, 1)
                    dve.wait_ge(x0_ready, KD)
                scale_h(0, 2 * q)
                scale_h(0, 2 * q + 1)
                rest_h(0, 2 * q)
                rest_h(0, 2 * q + 1)
            ffn(0)

            next_h(0, START[2])
            softplus()
            finish_mod(48, 72, 14)
            link(make_a(2))
            make_g(2)
            for t in range(CT):
                last = nc.vector.memset(xr[:, t, 0:3], 0.0)
            last.then_inc(xr_zero, 1)

            def att_step(i):
                if i < NU:
                    qt = i % NT
                    w = (qt + 1) * P
                    dve.wait_ge(s_done, i + 1)
                    if i >= 4:
                        dve.wait_ge(pt_done, i - 3)
                    nc.vector.tensor_tensor_reduce(out=att[:, i % 4, 0:w], in0=bank_s[:, 0:w],
                                                   in1=mask[:, S - w:S], scale=-1.0 / 8, scalar=3e38,
                                                   op0=ALU.add, op1=ALU.min,
                                                   accum_out=neg_max[:, i % 4, :]).then_inc(negs_done, 1)
                if 1 <= i <= NU:
                    u = i - 1
                    w = (u % NT + 1) * P
                    dve.wait_ge(exp_done, u + 1)
                    link(nc.vector.reciprocal(rden[:, u % 4, :], den[:, u % 4, :]))
                    nc.vector.tensor_scalar(att[:, u % 4, 0:w], att[:, u % 4, 0:w], rden[:, u % 4, :],
                                            None, ALU.mult).then_inc(p_ready, 1)
                if i % 8 == (7 + PV_LAG) % 8 and i >= 7 + PV_LAG:
                    p = (i - 7 - PV_LAG) // 8
                    dve.wait_ge(o_hi_done, p + 1)
                    nc.vector.tensor_tensor(mix_lo[:, p, :], bank_o[:, :], mix_hi[:, p, :].bitcast(F32),
                                            ALU.subtract).then_inc(o_lo_done, 1)

            def conv(t):
                dve.wait_ge(mix_evac, AT[6 + t // 2] + 1)
                if t >= 2:
                    dve.wait_ge(gate_done, 2 * t - 2)
                w = 8 + t
                link(nc.vector.tensor_scalar(xc[t % 2], xr[:, t, 0:S], cols_b[:, w:w + 1],
                                             cols_b[:, 24 + t:25 + t], ALU.mult, ALU.add))
                for tap in range(1, TAPS):
                    w += CT
                    last = nc.vector.scalar_tensor_tensor(xc[t % 2], xr[:, t, tap:tap + S],
                                                          cols_b[:, w:w + 1], xc[t % 2], ALU.mult, ALU.add)
                    if tap < TAPS - 1:
                        link(last)
                last.then_inc(conv_done, 1)

            def om_step(t):
                dve.wait_ge(lru_a_done, t + 1)
                link(nc.vector.tensor_tensor(om[t % 2], aa[t % 2], aa[t % 2], ALU.mult))
                nc.vector.scalar_tensor_tensor(om[t % 2], om[t % 2], 1.0, tmp[:, 1, :], ALU.add,
                                               ALU.mult).then_inc(om_done, 1)

            def scan(t):
                b = t % 2
                dve.wait_ge(tx_done, t + 1)
                dve.wait_ge(conv_done, t + 1)
                link(nc.vector.scalar_tensor_tensor(tx[b], tx[b], 1.0, xc[b], ALU.add, ALU.mult))
                dve.wait_ge(sqrt_done, t + 1)
                link(nc.vector.scalar_tensor_tensor(tx[b], tx[b], 0.5, om[b], ALU.mult, ALU.mult))
                nc.vector.tensor_tensor_scan(xr[:, t, 3:3 + S], aa[b], tx[b], 0.0, ALU.mult,
                                             ALU.add).then_inc(scan_done, 1)

            def gelu(t):
                dve.wait_ge(gsq_done, t + 1)
                link(nc.vector.tensor_scalar(tmp[:, 2, :], tmp[:, 2, :], 0.044715, 1.0, ALU.mult, ALU.add))
                nc.vector.tensor_tensor(tmp[:, 2, :], tmp[:, 2, :], gel[:, t, :], ALU.mult)\
                    .then_inc(gu_done, 1)

            def gelu_t(t):
                dve.wait_ge(gt_done, t + 1)
                nc.vector.scalar_tensor_tensor(gel[:, t, :], tmp[:, 2, :], 1.0, gel[:, t, :], ALU.add,
                                               ALU.mult).then_inc(gel_done, 1)

            def rec(t):
                dve.wait_ge(gel_done, t + 1)
                dve.wait_ge(scan_done, t + 1)
                nc.vector.scalar_tensor_tensor(gel[:, t, :], xr[:, t, 3:3 + S], 0.5, gel[:, t, :],
                                               ALU.mult, ALU.mult).then_inc(rec_f_done, 1)

            def rec_lo(t):
                dve.wait_ge(rec_hi_done, t + 1)
                nc.vector.tensor_tensor(mix_lo[:, 4 + t, :], gel[:, t, :], mix_hi[:, 4 + t, :].bitcast(F32),
                                        ALU.subtract).then_inc(rec_ready, 1)

            for hp in range(112):
                if hp in Y_AT:
                    if hp == Y_AT[0]:
                        dve.wait_ge(scan_done, 4)
                    add_y(1, Y_AT.index(hp))
                for e, arg in EVENTS.get(hp, ()):
                    if e == "att":
                        att_step(arg)
                    elif e == "conv":
                        conv(arg)
                    elif e == "om":
                        om_step(arg)
                    elif e == "scan":
                        scan(arg)
                    elif e == "gelu":
                        gelu(arg)
                    elif e == "gelu_t":
                        gelu_t(arg)
                    elif e == "rec":
                        rec(arg)
                    elif e == "rec_lo":
                        rec_lo(arg)
            add_y(1, 3)
            next_h(1, START[4])
            ffn(1)
            dve.wait_ge(rms_ready, 6)
            link(nc.vector.reciprocal(rms[:, 1, :], rms[:, 1, :]))
            dve.wait_ge(turned, 14)
            dve.wait_ge(out_tr, 8)
            for t in range(NT):
                for lo, hi, part in ((0, 768, y_out[:, t, 0:768]),
                                     (768, D, ps[6 + t // 2][:, (t % 2) * 256:(t % 2) * 256 + 256])):
                    nc.vector.scalar_tensor_tensor(x_out[:, t, lo:hi], part, rms[:, 1, t:t + 1],
                                                   x_out[:, t, lo:hi], ALU.mult, ALU.add)\
                        .then_inc(out_v, 1)


_INS = ["x", "c", "w_ada", "b_ada", "norm_gain", "ffn1_w_in", "ffn1_w_out", "mix_w_in", "conv_w", "conv_b",
        "lru_w_x", "lru_b_x", "lru_w_a", "lru_b_a", "lru_lambda", "mix_w_out", "ffn2_w_in", "ffn2_w_out"]


def kernel(**inputs):
    import numpy as _np
    import concourse.bacc as _bacc
    from concourse import mybir as _mybir
    from concourse.bass_utils import run_bass_kernel_spmd as _run

    nc = _bacc.Bacc("TRN2", target_bir_lowering=False, num_devices=1)
    arrays, args = {}, []
    for name in _INS:
        a = _np.ascontiguousarray(inputs[name])
        arrays[f"in_{name}"] = a
        ap = nc.dram_tensor(f"in_{name}", a.shape, _mybir.dt.from_np(a.dtype), kind="ExternalInput").ap()
        args.append(ap[0])
    out = nc.dram_tensor("out_y", (1, S, D), _mybir.dt.float32, kind="ExternalOutput").ap()
    build(nc, *args, out[0])
    r = _run(nc, [arrays], core_ids=[0])
    return r.results[0]["out_y"]
```
